# Optimizing a Trainium2 kernel written in Bass

```python
import math
import jax, jax.numpy as jnp
from jax import lax
import numpy as np

D_MODEL = 1024
BATCH = 1
SEQ = 512
DEPTH = 1

NSA_HEADS = 16
NSA_KV_GROUPS = 2
NSA_HEADS_PER_GROUP = NSA_HEADS // NSA_KV_GROUPS
NSA_HEAD_DIM = 64
CMP_BLOCK = 32
CMP_STRIDE = 16
CMP_HIDDEN = 256
SLC_BLOCK = 64
SLC_TOPN = 16
WINDOW = 512
Q_BLOCK = 128
ROPE_THETA = 500000.0
ROPE_DIM = NSA_HEAD_DIM // 4
FORCED_SCORE = 1.0e4

RET_HEADS = 8
RET_KEY_DIM = 64
RET_VAL_DIM = 128
RET_CHUNK = 128
RET_ROPE_THETA = 10000.0

D_FF = 2816
EPS = 1e-6
GN_EPS = 1e-5
NEG_INF = -1e30

NSA_Q_W = NSA_HEADS * NSA_HEAD_DIM
NSA_KV_W = NSA_KV_GROUPS * NSA_HEAD_DIM
NSA_GATE_W = 3 * NSA_HEADS
RET_QK_W = RET_HEADS * RET_KEY_DIM
RET_V_W = RET_HEADS * RET_VAL_DIM
IN_WIDTHS = (NSA_Q_W, NSA_KV_W, NSA_KV_W, NSA_KV_W, NSA_KV_W, NSA_KV_W, NSA_KV_W,
             NSA_GATE_W, RET_QK_W, RET_QK_W, RET_V_W, RET_V_W, 2 * D_MODEL)
D_IN = sum(IN_WIDTHS)


def _rmsnorm(x, g):
    xf = x.astype(jnp.float32)
    y = xf * lax.rsqrt(jnp.mean(xf * xf, axis=-1, keepdims=True) + EPS)
    return (y * g.astype(jnp.float32)).astype(x.dtype)

def _swiglu(x, w_gate, w_up, w_down):
    return (jax.nn.silu(x @ w_gate) * (x @ w_up)) @ w_down

def _rope(x, pos, rot_dim, theta):
    half = rot_dim // 2
    freqs = theta ** (-(jnp.arange(half, dtype=jnp.float32) * 2.0 / rot_dim))
    ang = pos.astype(jnp.float32)[:, None] * freqs[None, :]
    cos = jnp.cos(ang).astype(x.dtype)
    sin = jnp.sin(ang).astype(x.dtype)
    x1 = x[..., :half]
    x2 = x[..., half:rot_dim]
    return jnp.concatenate([x1 * cos - x2 * sin, x2 * cos + x1 * sin, x[..., rot_dim:]], axis=-1)

def _masked_softmax(s, mask):
    s = jnp.where(mask, s.astype(jnp.float32), NEG_INF)
    m = jnp.max(s, axis=-1, keepdims=True)
    p = jnp.where(mask, jnp.exp(s - m), 0.0)
    return p / jnp.maximum(jnp.sum(p, axis=-1, keepdims=True), 1e-20)

def _nsa(q, k_cmp, v_cmp, k_slc, v_slc, k_win, v_win, gates, pos_emb, ck_w1, ck_w2, cv_w1, cv_w2):
    B, G, Hg, S, dh = q.shape
    scale = dh ** -0.5
    pos = jnp.arange(S)
    q = _rope(q, pos, ROPE_DIM, ROPE_THETA)
    k_slc = _rope(k_slc, pos, ROPE_DIM, ROPE_THETA)
    k_win = _rope(k_win, pos, ROPE_DIM, ROPE_THETA)

    n_cmp = (S - CMP_BLOCK) // CMP_STRIDE + 1
    cmp_start = jnp.arange(n_cmp) * CMP_STRIDE
    cmp_end = cmp_start + CMP_BLOCK - 1
    cmp_idx = cmp_start[:, None] + jnp.arange(CMP_BLOCK)[None, :]

    def compress(tok, w1, w2):
        blk = tok[:, :, cmp_idx] + pos_emb
        blk = blk.reshape(B, G, n_cmp, CMP_BLOCK * dh)
        return jax.nn.gelu(blk @ w1) @ w2

    kc = _rope(compress(k_cmp, ck_w1, ck_w2), cmp_end, ROPE_DIM, ROPE_THETA)
    vc = compress(v_cmp, cv_w1, cv_w2)

    n_slc = S // SLC_BLOCK
    s_start = jnp.arange(n_slc) * SLC_BLOCK
    overlap = jnp.clip(jnp.minimum(cmp_start[:, None] + CMP_BLOCK, s_start[None, :] + SLC_BLOCK)
                       - jnp.maximum(cmp_start[:, None], s_start[None, :]), 0, None)
    cmp_to_slc = overlap.astype(jnp.float32) / CMP_BLOCK
    top_n = min(SLC_TOPN, n_slc)

    k_blocks = k_slc.reshape(B, G, n_slc, SLC_BLOCK, dh)
    v_blocks = v_slc.reshape(B, G, n_slc, SLC_BLOCK, dh)
    k_pad = jnp.pad(k_win, ((0, 0), (0, 0), (WINDOW, 0), (0, 0)))
    v_pad = jnp.pad(v_win, ((0, 0), (0, 0), (WINDOW, 0), (0, 0)))
    b_ix = jnp.arange(B)[:, None, None, None]
    g_ix = jnp.arange(G)[None, :, None, None]
    sb = jnp.arange(n_slc)

    def one_block(c):
        q0 = c * Q_BLOCK
        qc = lax.dynamic_slice_in_dim(q, q0, Q_BLOCK, axis=3)
        gc = lax.dynamic_slice_in_dim(gates, q0, Q_BLOCK, axis=3)
        t = q0 + jnp.arange(Q_BLOCK)

        s_c = jnp.einsum('bghqd,bgnd->bghqn', qc, kc) * scale
        p_c = _masked_softmax(s_c, cmp_end[None, :] <= t[:, None])
        o_c = jnp.einsum('bghqn,bgnd->bghqd', p_c.astype(vc.dtype), vc)

        imp = jnp.einsum('bghqn,ns->bgqs', p_c, cmp_to_slc)
        cur = t // SLC_BLOCK
        forced = (sb[None, :] == 0) | (sb[None, :] == cur[:, None]) | (sb[None, :] == cur[:, None] - 1)
        future = sb[None, :] > cur[:, None]
        imp = jnp.where(forced, FORCED_SCORE, jnp.where(future, -FORCED_SCORE, imp))
        _, sel = lax.top_k(imp, top_n)
        k_sel = k_blocks[b_ix, g_ix, sel]
        v_sel = v_blocks[b_ix, g_ix, sel]
        kpos = sel[..., None] * SLC_BLOCK + jnp.arange(SLC_BLOCK)
        s_s = jnp.einsum('bghqd,bgqnkd->bghqnk', qc, k_sel) * scale
        s_s = s_s.reshape(B, G, Hg, Q_BLOCK, top_n * SLC_BLOCK)
        mask_s = (kpos <= t[:, None, None]).reshape(B, G, 1, Q_BLOCK, top_n * SLC_BLOCK)
        p_s = _masked_softmax(s_s, mask_s).reshape(B, G, Hg, Q_BLOCK, top_n, SLC_BLOCK)
        o_s = jnp.einsum('bghqnk,bgqnkd->bghqd', p_s.astype(v_sel.dtype), v_sel)

        kw = lax.dynamic_slice_in_dim(k_pad, q0, WINDOW + Q_BLOCK, axis=2)
        vw = lax.dynamic_slice_in_dim(v_pad, q0, WINDOW + Q_BLOCK, axis=2)
        wpos = q0 - WINDOW + jnp.arange(WINDOW + Q_BLOCK)
        dist = t[:, None] - wpos[None, :]
        mask_w = (wpos[None, :] >= 0) & (dist >= 0) & (dist < WINDOW)
        s_w = jnp.einsum('bghqd,bgkd->bghqk', qc, kw) * scale
        p_w = _masked_softmax(s_w, mask_w)
        o_w = jnp.einsum('bghqk,bgkd->bghqd', p_w.astype(vw.dtype), vw)

        return gc[..., 0:1] * o_c + gc[..., 1:2] * o_s + gc[..., 2:3] * o_w

    out = lax.map(one_block, jnp.arange(S // Q_BLOCK))
    return out.transpose(1, 0, 4, 2, 3, 5).reshape(B, S, G * Hg * dh)

def _retention(q, k, v, gn_gain):
    B, H, S, dk = q.shape
    dv = v.shape[-1]
    C = RET_CHUNK
    N = S // C
    dt = q.dtype
    pos = jnp.arange(S)
    q = _rope(q, pos, dk, RET_ROPE_THETA) * (dk ** -0.5)
    k = _rope(k, pos, dk, RET_ROPE_THETA)
    log_g = jnp.log(1.0 - 2.0 ** (-5.0 - jnp.arange(H, dtype=jnp.float32)))
    i = jnp.arange(C, dtype=jnp.float32)
    diff = i[:, None] - i[None, :]
    decay = jnp.where(diff >= 0, jnp.exp(jnp.maximum(diff, 0.0) * log_g[:, None, None]), 0.0)
    zeta = jnp.exp((C - 1.0 - i)[None, :] * log_g[:, None])
    xi = jnp.exp((i + 1.0)[None, :] * log_g[:, None])
    g_chunk = jnp.exp(C * log_g)

    qc = q.reshape(B, H, N, C, dk)
    kc = k.reshape(B, H, N, C, dk)
    vc = v.reshape(B, H, N, C, dv)
    inner = jnp.einsum('bhncd,bhnkd->bhnck', qc, kc) * decay[None, :, None].astype(dt)
    o_inner = jnp.einsum('bhnck,bhnke->bhnce', inner, vc)
    kv = jnp.einsum('bhncd,bhnce->nbhde', kc * zeta[None, :, None, :, None].astype(dt), vc)
    kv = kv.astype(jnp.float32)

    def step(R, kv_n):
        return g_chunk[None, :, None, None] * R + kv_n, R

    _, R_prev = lax.scan(step, jnp.zeros((B, H, dk, dv), jnp.float32), kv)
    o_cross = jnp.einsum('bhncd,nbhde->bhnce',
                         (qc * xi[None, :, None, :, None].astype(dt)).astype(jnp.float32), R_prev)
    o = (o_inner.astype(jnp.float32) + o_cross).reshape(B, H, S, dv)
    mu = jnp.mean(o, axis=-1, keepdims=True)
    var = jnp.mean(jnp.square(o - mu), axis=-1, keepdims=True)
    on = (o - mu) * lax.rsqrt(var + GN_EPS) * gn_gain.astype(jnp.float32)[None, :, None, :]
    return on.astype(dt).transpose(0, 2, 1, 3).reshape(B, S, H * dv)

def first_inputs(seed: int = 0) -> dict:
    key = jax.random.key(seed)
    ks = jax.random.split(key, 24)
    f32 = jnp.float32

    def w(k, shape, fan_in):
        return jax.random.normal(k, shape, f32) * (fan_in ** -0.5)

    def gain(k, shape):
        return 1.0 + 0.02 * jax.random.normal(k, shape, f32)

    L = DEPTH
    return {
        "x": jax.random.normal(ks[0], (BATCH, SEQ, D_MODEL), f32),
        "ffn1_norm": gain(ks[1], (L, D_MODEL)),
        "ffn1_w_gate": w(ks[2], (L, D_MODEL, D_FF), D_MODEL),
        "ffn1_w_up": w(ks[3], (L, D_MODEL, D_FF), D_MODEL),
        "ffn1_w_down": w(ks[4], (L, D_FF, D_MODEL), D_FF),
        "mix_norm": gain(ks[5], (L, D_MODEL)),
        "w_in": w(ks[6], (L, D_MODEL, D_IN), D_MODEL),
        "cmp_pos_emb": 0.1 * jax.random.normal(ks[7], (L, CMP_BLOCK, NSA_HEAD_DIM), f32),
        "cmp_k_w1": w(ks[8], (L, CMP_BLOCK * NSA_HEAD_DIM, CMP_HIDDEN), CMP_BLOCK * NSA_HEAD_DIM),
        "cmp_k_w2": w(ks[9], (L, CMP_HIDDEN, NSA_HEAD_DIM), CMP_HIDDEN),
        "cmp_v_w1": w(ks[10], (L, CMP_BLOCK * NSA_HEAD_DIM, CMP_HIDDEN), CMP_BLOCK * NSA_HEAD_DIM),
        "cmp_v_w2": w(ks[11], (L, CMP_HIDDEN, NSA_HEAD_DIM), CMP_HIDDEN),
        "ret_gn_gain": gain(ks[12], (L, RET_HEADS, RET_VAL_DIM)),
        "w_branch_nsa": w(ks[13], (L, NSA_Q_W, D_MODEL), NSA_Q_W),
        "w_branch_ret": w(ks[14], (L, RET_V_W, D_MODEL), RET_V_W),
        "w_out": w(ks[15], (L, D_MODEL, D_MODEL), D_MODEL),
        "ffn2_norm": gain(ks[16], (L, D_MODEL)),
        "ffn2_w_gate": w(ks[17], (L, D_MODEL, D_FF), D_MODEL),
        "ffn2_w_up": w(ks[18], (L, D_MODEL, D_FF), D_MODEL),
        "ffn2_w_down": w(ks[19], (L, D_FF, D_MODEL), D_FF),
        "final_norm": gain(ks[20], (D_MODEL,)),
    }

def first_block(x, ffn1_norm, ffn1_w_gate, ffn1_w_up, ffn1_w_down, mix_norm, w_in,
              cmp_pos_emb, cmp_k_w1, cmp_k_w2, cmp_v_w1, cmp_v_w2, ret_gn_gain,
              w_branch_nsa, w_branch_ret, w_out, ffn2_norm, ffn2_w_gate, ffn2_w_up,
              ffn2_w_down, final_norm):
    B, S, _ = x.shape
    G, Hg, dh = NSA_KV_GROUPS, NSA_HEADS_PER_GROUP, NSA_HEAD_DIM
    split_points = [int(p) for p in np.cumsum(IN_WIDTHS)[:-1]]

    def nsa_heads(t):
        return t.reshape(B, S, G, Hg, dh).transpose(0, 2, 3, 1, 4)

    def nsa_kv(t):
        return t.reshape(B, S, G, dh).transpose(0, 2, 1, 3)

    def ret_heads(t, d):
        return t.reshape(B, S, RET_HEADS, d).transpose(0, 2, 1, 3)

    for layer in range(DEPTH):
        h = _rmsnorm(x, ffn1_norm[layer])
        x = x + 0.5 * _swiglu(h, ffn1_w_gate[layer], ffn1_w_up[layer], ffn1_w_down[layer])

        h = _rmsnorm(x, mix_norm[layer])
        proj = h @ w_in[layer]
        (q_a, kc_a, vc_a, ks_a, vs_a, kw_a, vw_a, g_a,
         q_r, k_r, v_r, g_r, g_merge) = jnp.split(proj, split_points, axis=-1)

        nsa_gates = jax.nn.sigmoid(g_a.reshape(B, S, G, Hg, 3).transpose(0, 2, 3, 1, 4))
        a_out = _nsa(nsa_heads(q_a), nsa_kv(kc_a), nsa_kv(vc_a), nsa_kv(ks_a), nsa_kv(vs_a),
                     nsa_kv(kw_a), nsa_kv(vw_a), nsa_gates, cmp_pos_emb[layer],
                     cmp_k_w1[layer], cmp_k_w2[layer], cmp_v_w1[layer], cmp_v_w2[layer])
        r_out = _retention(ret_heads(q_r, RET_KEY_DIM), ret_heads(k_r, RET_KEY_DIM),
                           ret_heads(v_r, RET_VAL_DIM), ret_gn_gain[layer])
        r_out = jax.nn.silu(g_r) * r_out

        gate_a, gate_r = jnp.split(jax.nn.sigmoid(g_merge), 2, axis=-1)
        mixed = gate_a * (a_out @ w_branch_nsa[layer]) + gate_r * (r_out @ w_branch_ret[layer])
        x = x + mixed @ w_out[layer]

        h = _rmsnorm(x, ffn2_norm[layer])
        x = x + 0.5 * _swiglu(h, ffn2_w_gate[layer], ffn2_w_up[layer], ffn2_w_down[layer])

    return _rmsnorm(x, final_norm)


CHUNK = 64
D_MIX = D_MODEL
DIFF_HEADS = 4
DIFF_QK_DIM = 64
DIFF_V_DIM = 2 * DIFF_QK_DIM
DIFF_WIDTH = DIFF_HEADS * DIFF_V_DIM
MLA_HEADS = 4
MLA_Q_RANK = 256
MLA_KV_RANK = 128
MLA_NOPE_DIM = 128
MLA_ROPE_DIM = 64
MLA_QK_DIM = MLA_NOPE_DIM + MLA_ROPE_DIM
MLA_V_DIM = 128
MLA_WIDTH = MLA_HEADS * MLA_V_DIM
ROPE_THETA_2 = 10000.0
REL_BUCKETS = 32
REL_MAX_DIST = 128
RMS_EPS = 1e-6
NEG_INF_2 = -1e30
COL_DIFF_Q = DIFF_HEADS * 2 * DIFF_QK_DIM
COL_DIFF_K = DIFF_HEADS * 2 * DIFF_QK_DIM
COL_DIFF_V = DIFF_WIDTH
COL_MLA_CQ = MLA_Q_RANK
COL_MLA_CKV = MLA_KV_RANK
COL_MLA_KR = MLA_ROPE_DIM
COL_GATE = D_MIX
IN_COLS = COL_DIFF_Q + COL_DIFF_K + COL_DIFF_V + COL_MLA_CQ + COL_MLA_CKV + COL_MLA_KR + COL_GATE


def _rms_norm(x, g):
    xf = x.astype(jnp.float32)
    y = xf * lax.rsqrt(jnp.mean(xf * xf, axis=-1, keepdims=True) + RMS_EPS)
    return (y * g.astype(jnp.float32)).astype(x.dtype)

def _rope_2(x, cos, sin):
    x1, x2 = jnp.split(x, 2, axis=-1)
    return jnp.concatenate([x1 * cos - x2 * sin, x2 * cos + x1 * sin], axis=-1).astype(x.dtype)

def _t5_bucket(rel):
    nb = REL_BUCKETS // 2
    max_exact = nb // 2
    ret = jnp.where(rel > 0, nb, 0)
    n = jnp.abs(rel)
    nf = jnp.maximum(n, 1).astype(jnp.float32)
    large = max_exact + (jnp.log(nf / max_exact) / math.log(REL_MAX_DIST / max_exact)
                         * (nb - max_exact)).astype(jnp.int32)
    large = jnp.minimum(large, nb - 1)
    return ret + jnp.where(n < max_exact, n, large)

def second_inputs(seed: int = 0) -> dict:
    key = jax.random.key(seed)
    ks = jax.random.split(key, 24)
    f32 = jnp.float32
    nrm = lambda k, shape, s: jax.random.normal(k, shape, f32) * s
    gain = lambda k, shape: 1.0 + 0.1 * jax.random.normal(k, shape, f32)
    x = jax.random.normal(ks[0], (BATCH, SEQ, D_MODEL), f32)
    c = jax.random.normal(ks[1], (BATCH, D_MODEL), f32)
    offset = jax.random.randint(ks[2], (BATCH, 1), 0, 1024, dtype=jnp.int32) * CHUNK
    positions = (offset + jnp.arange(SEQ, dtype=jnp.int32)[None, :]).astype(jnp.int32)
    return {
        "x": x,
        "c": c,
        "positions": positions,
        "rel_bias": nrm(ks[3], (REL_BUCKETS, DIFF_HEADS), 0.5),
        "ada_w": nrm(ks[4], (DEPTH, D_MODEL, 3 * D_MODEL), 0.5 * D_MODEL ** -0.5),
        "ada_b": nrm(ks[5], (DEPTH, 3 * D_MODEL), 0.02),
        "norm_g": gain(ks[6], (DEPTH, D_MODEL)),
        "w_in": nrm(ks[7], (DEPTH, D_MODEL, IN_COLS), D_MODEL ** -0.5),
        "diff_q_norm": gain(ks[8], (DEPTH, DIFF_QK_DIM)),
        "diff_k_norm": gain(ks[9], (DEPTH, DIFF_QK_DIM)),
        "diff_lambda": nrm(ks[10], (DEPTH, 4, DIFF_QK_DIM), 0.1),
        "diff_sub_norm": gain(ks[11], (DEPTH, DIFF_V_DIM)),
        "mla_q_a_norm": gain(ks[12], (DEPTH, MLA_Q_RANK)),
        "mla_kv_a_norm": gain(ks[13], (DEPTH, MLA_KV_RANK)),
        "w_uq": nrm(ks[14], (DEPTH, MLA_Q_RANK, MLA_HEADS * MLA_QK_DIM), MLA_Q_RANK ** -0.5),
        "w_uk": nrm(ks[15], (DEPTH, MLA_KV_RANK, MLA_HEADS * MLA_NOPE_DIM), MLA_KV_RANK ** -0.5),
        "w_uv": nrm(ks[16], (DEPTH, MLA_KV_RANK, MLA_HEADS * MLA_V_DIM), MLA_KV_RANK ** -0.5),
        "mla_q_norm": gain(ks[17], (DEPTH, MLA_QK_DIM)),
        "mla_k_norm": gain(ks[18], (DEPTH, MLA_QK_DIM)),
        "w_out": nrm(ks[19], (DEPTH, D_MIX, D_MODEL), D_MIX ** -0.5),
    }

def _layer(x, c, positions, rel_bias, layer_idx, ada_w, ada_b, norm_g, w_in,
           diff_q_norm, diff_k_norm, diff_lambda, diff_sub_norm,
           mla_q_a_norm, mla_kv_a_norm, w_uq, w_uk, w_uv, mla_q_norm, mla_k_norm, w_out):
    B, S, _ = x.shape
    mod = jax.nn.silu(c) @ ada_w + ada_b
    shift, scale, gate = jnp.split(mod, 3, axis=-1)
    h = _rms_norm(x, norm_g) * (1.0 + scale[:, None, :]) + shift[:, None, :]

    proj = h @ w_in
    cuts = np.cumsum([COL_DIFF_Q, COL_DIFF_K, COL_DIFF_V, COL_MLA_CQ, COL_MLA_CKV, COL_MLA_KR])
    dq, dk, dv, cq, ckv, kr, g = jnp.split(proj, [int(v) for v in cuts], axis=-1)

    dq = _rms_norm(dq.reshape(B, S, DIFF_HEADS, 2, DIFF_QK_DIM), diff_q_norm)
    dk = _rms_norm(dk.reshape(B, S, DIFF_HEADS, 2, DIFF_QK_DIM), diff_k_norm)
    dv = dv.reshape(B, S, DIFF_HEADS, DIFF_V_DIM)
    lam_init = 0.8 - 0.6 * math.exp(-0.3 * (layer_idx - 1))
    lam_f = diff_lambda.astype(jnp.float32)
    lam = (jnp.exp(jnp.sum(lam_f[0] * lam_f[1])) - jnp.exp(jnp.sum(lam_f[2] * lam_f[3]))
           + lam_init)

    half = MLA_ROPE_DIM // 2
    inv_freq = ROPE_THETA_2 ** (-jnp.arange(half, dtype=jnp.float32) / half)
    ang = positions.astype(jnp.float32)[:, :, None] * inv_freq
    cos, sin = jnp.cos(ang), jnp.sin(ang)
    q_m = (_rms_norm(cq, mla_q_a_norm) @ w_uq).reshape(B, S, MLA_HEADS, MLA_QK_DIM)
    q_nope, q_pe = q_m[..., :MLA_NOPE_DIM], q_m[..., MLA_NOPE_DIM:]
    q_pe = _rope_2(q_pe, cos[:, :, None, :], sin[:, :, None, :])
    ckv_n = _rms_norm(ckv, mla_kv_a_norm)
    k_nope = (ckv_n @ w_uk).reshape(B, S, MLA_HEADS, MLA_NOPE_DIM)
    v_m = (ckv_n @ w_uv).reshape(B, S, MLA_HEADS, MLA_V_DIM)
    k_pe = jnp.broadcast_to(_rope_2(kr, cos, sin)[:, :, None, :], (B, S, MLA_HEADS, MLA_ROPE_DIM))
    q_m = _rms_norm(jnp.concatenate([q_nope, q_pe], axis=-1), mla_q_norm)
    k_m = _rms_norm(jnp.concatenate([k_nope, k_pe], axis=-1), mla_k_norm)

    key_chunk = positions // CHUNK
    diff_scale = DIFF_QK_DIM ** -0.5
    mla_scale = MLA_QK_DIM ** -0.5

    def attend_block(i):
        q0 = i * Q_BLOCK
        qpos = lax.dynamic_slice_in_dim(positions, q0, Q_BLOCK, axis=1)
        allowed = key_chunk[:, None, :] <= (qpos // CHUNK)[:, :, None]
        bucket = _t5_bucket(positions[:, None, :] - qpos[:, :, None])
        bias = jnp.transpose(rel_bias[bucket], (0, 3, 1, 2)).astype(jnp.float32)
        dq_b = lax.dynamic_slice_in_dim(dq, q0, Q_BLOCK, axis=1)
        logit_d = jnp.einsum('bqhcd,bkhcd->bchqk', dq_b, dk).astype(jnp.float32) * diff_scale
        logit_d = jnp.where(allowed[:, None, None], logit_d + bias[:, None], NEG_INF_2)
        p_d = jax.nn.softmax(logit_d, axis=-1)
        attn_d = p_d[:, 0] - lam * p_d[:, 1]
        o_d = jnp.einsum('bhqk,bkhd->bqhd', attn_d.astype(dv.dtype), dv)
        o_d = _rms_norm(o_d, diff_sub_norm) * (1.0 - lam_init)
        q_b = lax.dynamic_slice_in_dim(q_m, q0, Q_BLOCK, axis=1)
        logit_m = jnp.einsum('bqhd,bkhd->bhqk', q_b, k_m).astype(jnp.float32) * mla_scale
        logit_m = jnp.where(allowed[:, None], logit_m, NEG_INF_2)
        p_m = jax.nn.softmax(logit_m, axis=-1)
        o_m = jnp.einsum('bhqk,bkhd->bqhd', p_m.astype(v_m.dtype), v_m)
        return jnp.concatenate([o_d.reshape(B, Q_BLOCK, DIFF_WIDTH),
                                o_m.reshape(B, Q_BLOCK, MLA_WIDTH)], axis=-1)

    n_blocks = S // Q_BLOCK
    mixed = lax.map(attend_block, jnp.arange(n_blocks, dtype=jnp.int32))
    mixed = jnp.transpose(mixed, (1, 0, 2, 3)).reshape(B, S, D_MIX)
    out = (mixed * jax.nn.silu(g)) @ w_out
    return x + gate[:, None, :] * out

def second_block(x, c, positions, rel_bias, ada_w, ada_b, norm_g, w_in, diff_q_norm, diff_k_norm,
              diff_lambda, diff_sub_norm, mla_q_a_norm, mla_kv_a_norm, w_uq, w_uk, w_uv,
              mla_q_norm, mla_k_norm, w_out):
    for l in range(DEPTH):
        x = _layer(x, c, positions, rel_bias, l + 1, ada_w[l], ada_b[l], norm_g[l], w_in[l],
                   diff_q_norm[l], diff_k_norm[l], diff_lambda[l], diff_sub_norm[l],
                   mla_q_a_norm[l], mla_kv_a_norm[l], w_uq[l], w_uk[l], w_uv[l],
                   mla_q_norm[l], mla_k_norm[l], w_out[l])
    return x


def setup_inputs(seed=0):
    out = dict(first_inputs(seed))
    for name, value in second_inputs(seed + 1).items():
        if name != "x":
            out[name + "_2"] = value
    return out


def reference(
    x, ffn1_norm, ffn1_w_gate, ffn1_w_up, ffn1_w_down, mix_norm, w_in, cmp_pos_emb, cmp_k_w1,
    cmp_k_w2, cmp_v_w1, cmp_v_w2, ret_gn_gain, w_branch_nsa, w_branch_ret, w_out, ffn2_norm,
    ffn2_w_gate, ffn2_w_up, ffn2_w_down, final_norm, c_2, positions_2, rel_bias_2, ada_w_2,
    ada_b_2, norm_g_2, w_in_2, diff_q_norm_2, diff_k_norm_2, diff_lambda_2, diff_sub_norm_2,
    mla_q_a_norm_2, mla_kv_a_norm_2, w_uq_2, w_uk_2, w_uv_2, mla_q_norm_2, mla_k_norm_2,
    w_out_2,
):
    x = first_block(
        x, ffn1_norm, ffn1_w_gate, ffn1_w_up, ffn1_w_down, mix_norm, w_in, cmp_pos_emb,
        cmp_k_w1, cmp_k_w2, cmp_v_w1, cmp_v_w2, ret_gn_gain, w_branch_nsa, w_branch_ret, w_out,
        ffn2_norm, ffn2_w_gate, ffn2_w_up, ffn2_w_down, final_norm,
    )
    return second_block(
        x, c_2, positions_2, rel_bias_2, ada_w_2, ada_b_2, norm_g_2, w_in_2, diff_q_norm_2,
        diff_k_norm_2, diff_lambda_2, diff_sub_norm_2, mla_q_a_norm_2, mla_kv_a_norm_2, w_uq_2,
        w_uk_2, w_uv_2, mla_q_norm_2, mla_k_norm_2, w_out_2,
    )


_drawn_inputs = setup_inputs


def setup_inputs(seed=0):
    import zlib

    import numpy as np

    out = dict(_drawn_inputs(seed))
    spreads = {}
    factors = {'ffn1_norm': 5.458,
     'mix_norm': 4.074,
     'cmp_pos_emb': 3.727,
     'ret_gn_gain': 8.0,
     'ffn2_norm': 7.522,
     'final_norm': 2.933,
     'rel_bias_2': 3.162,
     'ada_b_2': 4.879,
     'norm_g_2': 3.673,
     'diff_q_norm_2': 8.0,
     'diff_k_norm_2': 8.0,
     'diff_lambda_2': 5.944,
     'diff_sub_norm_2': 4.576,
     'mla_q_a_norm_2': 8.0,
     'mla_kv_a_norm_2': 8.0,
     'w_uq_2': 3.551,
     'w_uk_2': 3.914,
     'mla_q_norm_2': 8.0,
     'mla_k_norm_2': 8.0}
    for name, (base, spread) in spreads.items():
        noise = np.random.default_rng([zlib.crc32(name.encode()), seed]).standard_normal(out[name].shape)
        drawn = base * np.exp(spread * noise) if base else spread * noise
        out[name] = __import__('jax').numpy.asarray(drawn.astype(out[name].dtype))
    for name, factor in factors.items():
        out[name] = (out[name] * factor).astype(out[name].dtype)
    return out
```

```python
from contextlib import ExitStack
import math

import numpy as np
import concourse.bass as bass
from concourse import mybir

F32 = mybir.dt.float32
F32R = mybir.dt.float32r
I32 = mybir.dt.int32
ALU = mybir.AluOpType
ACT = mybir.ActivationFunctionType
AX = mybir.AxisListType.X

P = 128
S = 512
D = 1024
KD = D // P
NT = S // P
FF = 2816
KF = FF // P
HALF_F = KF // 2
EPS = 1e-6
GN_EPS = 1e-5
NEG = -1e30
HEADS = 16
GROUPS = 2
DH = 64
NCMP = (S - 32) // 16 + 1
NCP = 32
NROW = NCP + NCMP
RH = 8
SCALE = DH ** -0.5
MLA_SCALE = 192 ** -0.5
LAM_INIT = 0.8 - 0.6 * math.exp(-0.3 * 0)

W_Q, W_KC, W_VC, W_KS, W_VS, W_KW, W_VW, W_G = 0, 1024, 1152, 1280, 1408, 1536, 1664, 1792
W_RQ, W_RK, W_RV, W_RG, W_GM = 1840, 2352, 2864, 3888, 4912
Z_DQ, Z_DK, Z_DV, Z_CQ, Z_CKV, Z_KR, Z_G = 0, 512, 1024, 1536, 1792, 1920, 1984

STEP_BUCKET = list(range(15, -1, -1)) + list(range(17, 32))
STEP_AT = [-3.0e8, -90, -63, -45, -31, -22, -15, -11, -7, -6, -5, -4, -3, -2, -1, 0,
           1, 2, 3, 4, 5, 6, 7, 8, 12, 16, 23, 32, 46, 64, 91]
NSTEP = 32

C_ID, C_ONE, C_ROTN, C_ROTR, C_CAUS = (128 * i for i in range(5))
C_COSN, C_SINN, C_COSR, C_SINR = (640 + 512 * i for i in range(4))
C_CM01 = 640 + 2048
C_CADD = C_CM01 + 128
C_PERM = C_CADD + 128
C_MISC = C_PERM + 128
C_HALF = C_MISC + 8
C_BLK = C_HALF + 64
C_END = C_HALF + 256

(G_F1, G_MIX, G_F2, G_FIN, G_N2, G_GN) = (8 * i for i in range(6))
G_DQ, G_DK, G_SUB, G_QA, G_KVA, G_QN, G_QP, G_KN, G_KP = 48, 49, 50, 51, 53, 54, 55, 56, 57
G_C, G_ADAB, G_MOD, G_LAM, G_EPS, G_GNEPS, G_MISC = 64, 72, 96, 120, 124, 125, 126
G_END = 132


def constants():
    c = np.zeros((P, C_END), np.float32)
    c[:, C_ID:C_ID + P] = np.eye(P)
    c[:, C_ONE:C_ONE + P] = 1.0
    c[:64, C_HALF:C_HALF + P] = 1.0
    c[64:, C_HALF + P:C_HALF + 2 * P] = 1.0
    for b in (0, 64):
        for half, col in ((8, C_ROTN), (32, C_ROTR)):
            for i in range(half):
                c[b + i + half, col + b + i] = -1.0
                c[b + i, col + b + i + half] = 1.0
    t = np.arange(S, dtype=np.float32)
    for half, rot, theta, cc, cs in ((8, 16, 500000.0, C_COSN, C_SINN), (32, 64, 10000.0, C_COSR, C_SINR)):
        f = (np.float32(theta) ** (-(np.arange(half, dtype=np.float32) * np.float32(2.0) / np.float32(rot)))).astype(np.float32)
        ang = (t[None, :] * f[:, None]).astype(np.float32).astype(np.float64)
        c[:, cc:cc + S] = 1.0
        for b in (0, 64):
            for o in (0, half):
                c[b + o:b + o + half, cc:cc + S] = np.cos(ang)
                c[b + o:b + o + half, cs:cs + S] = np.sin(ang)
    k = np.arange(P)
    c[:, C_CAUS:C_CAUS + P] = np.where(k[None, :] <= k[:, None], 0.0, NEG)
    for j in range(NT):
        q = j * P + np.arange(P)
        seen = np.zeros((P, NCP), np.float32)
        seen[:, :NCMP] = (16 * np.arange(NCMP)[None, :] + 31) <= q[:, None]
        c[:, C_CM01 + j * NCP:C_CM01 + (j + 1) * NCP] = seen
        c[:, C_CADD + j * NCP:C_CADD + (j + 1) * NCP] = np.where(seen > 0, 0.0, NEG)
    for rep in range(4):
        for i, b in enumerate(STEP_BUCKET):
            c[b, C_PERM + rep * NSTEP + i] += 1.0
            if i:
                c[STEP_BUCKET[i - 1], C_PERM + rep * NSTEP + i] -= 1.0
            c[rep * NSTEP + i, C_MISC] = STEP_AT[i]
    c[:, C_MISC + 1] = (10000.0 ** (-((np.arange(P) % 32).astype(np.float32) / np.float32(32)).astype(np.float64))).astype(np.float32)
    lg = np.log(1.0 - 2.0 ** (-5.0 - np.arange(RH)))
    d = np.arange(S)[None, :] - np.arange(P)[:, None]
    decay = np.where(d[None] >= 0, np.exp(np.maximum(d, 0)[None] * lg[:, None, None]), 0.0) * SCALE
    return c, decay.astype(np.float32)


def build(nc, A, out):
    ctx = ExitStack()
    with ctx:
        ctx.enter_context(nc.allow_non_contiguous_dma(reason="short vectors of one number a feature"))
        names = {}

        def sem(name):
            if name not in names:
                names[name] = ctx.enter_context(nc.semaphore(name))
            return names[name]

        base = [16512]

        def at(name, shape, dt, offset=None):
            size = int(np.prod(shape[1:])) * 4
            if offset is None:
                offset = base[0]
                base[0] += (size + 31) // 32 * 32
            assert offset + size <= 229344, (name, offset + size)
            return nc.alloc_sbuf_tensor_at(name, shape, dt, offset=offset)

        cst = at("cst", [P, C_END], F32)
        col = at("col", [P, G_END], F32)
        mstat = at("mstat", [P, 2, 8], F32)
        x = at("x", [P, KD, S], F32)
        h_hi = at("h_hi", [P, KD, S], F32R)
        h_lo = at("h_lo", [P, KD, S], F32R)
        w_raw = [at(f"w_raw{i}", [P, 2048], F32) for i in range(2)]
        w_hi = [at(f"w_hi{i}", [P, 2048], F32R) for i in range(2)]
        w_lo = [at(f"w_lo{i}", [P, 2048], F32R) for i in range(2)]
        ARENA = base[0]
        KB = 1024
        u_hi = at("u_hi", [P, HALF_F, S], F32R, ARENA)
        u_lo = at("u_lo", [P, HALF_F, S], F32R, ARENA + 22 * KB)
        silu = [at(f"silu{i}", [P, S], F32, ARENA + (44 + 2 * i) * KB) for i in range(2)]
        act_f = at("act_f", [P, S], F32, ARENA + 48 * KB)
        ada_sum = at("ada_sum", [P, 3 * D], F32, ARENA + 50 * KB)
        ada_w = [at(f"ada_w{i}", [P, 3 * D // 2], F32, ARENA + 62 * KB + i * 6 * KB) for i in range(3)]
        sq = [at(f"sq{i}", [P, S], F32, ARENA + (84 + 2 * i) * KB) for i in range(2)]
        std = at("std", [P, S], F32, ARENA + 88 * KB)
        rs = at("rs", [P, S], F32, ARENA + 90 * KB)
        tmp = at("tmp", [P, S], F32, ARENA + 92 * KB)
        tmp2 = at("tmp2", [P, S], F32, ARENA + 94 * KB)
        sqsum = at("sqsum", [P, S], F32, ARENA + 80 * KB)
        sqg = [at(f"sqg{i}", [P, S], F32, ARENA + (60 + 2 * i) * KB) for i in range(2)]
        sqgsum = at("sqgsum", [P, S], F32, ARENA + 64 * KB)
        rs2 = at("rs2", [P, S], F32, ARENA + 66 * KB)
        xin = at("xin", [P, NT, D], F32, ARENA)
        a_hi = at("a_hi", [P, KD, S], F32R, ARENA)
        a_lo = at("a_lo", [P, KD, S], F32R, ARENA + 16 * KB)
        N0 = ARENA + 32 * KB
        qT = at("qT", [P, KD, S], F32, N0)
        kv_c = at("kv_c", [P, 2, S], F32, N0 + 16 * KB)
        kv_s = at("kv_s", [P, 2, S], F32, N0 + 20 * KB)
        kz = at("kz", [P, 2, GROUPS, 2, S], F32, N0 + 24 * KB)
        vtok = at("vtok", [P, NT, 256], F32, N0 + 40 * KB)
        gates = at("gates", [P, NT, 48], F32, N0 + 44 * KB)
        T2 = at("T2", [P, 2, GROUPS, S], F32, ARENA)
        w1 = at("w1", [P, 16, 256], F32, ARENA + 8 * KB)
        w1v = at("w1v", [P, 8, 256], F32, ARENA + 84 * KB)
        posT = at("posT", [P, 16], F32, ARENA + 24 * KB)
        pos_tok = at("pos_tok", [16, P], F32, ARENA + 24 * KB + 64)
        hid = at("hid", [NROW, 2, 256], F32, ARENA + 25 * KB)
        gl = [at(f"gl{i}", [NROW, 256], F32, ARENA + (27 + i) * KB) for i in range(2)]
        hidT = at("hidT", [P, 2, 2, GROUPS, NCP], F32, ARENA + 29 * KB)
        w2 = at("w2", [P, 2, 2, 128], F32, ARENA + 30 * KB)
        hrep = at("hrep", [P, 2, GROUPS, 4, NCP], F32, N0 + 20 * KB)
        pbias = at("pbias", [1, 2, 256], F32, N0 + 22 * KB)
        kcz = at("kcz", [P, 2, GROUPS, NCP], F32, N0 + 45 * KB)
        kcr = at("kcr", [P, GROUPS, NCP], F32, N0 + 45 * KB + 512)
        vcz = at("vcz", [P, 4, GROUPS, DH], F32, ARENA + 78 * KB)
        pTc = at("pTc", [P, NT, 4, P], F32, N0 + 16 * KB)
        sc = at("sc", [P, HEADS, NCP], F32, ARENA + 80 * KB)
        sstat = at("sstat", [P, 3, HEADS], F32, ARENA + 82 * KB)
        Pm = [at(f"Pm{i}", [P, 2, S], F32, ARENA + (80 + 4 * i) * KB) for i in range(2)]
        PTm = [at(f"PTm{i}", [P, 2, S], F32, ARENA + (88 + 4 * i) * KB) for i in range(2)]
        rq = at("rq", [P, 4, S], F32, N0)
        rkz = at("rkz", [P, RH, S], F32, N0 + 8 * KB)
        rk = at("rk", [P, 4, S], F32, ARENA + 82 * KB)
        rv = at("rv", [P, NT, 1024], F32, N0 + 24 * KB)
        dec = [at(f"dec{i}", [P, S], F32, N0 + (40 + 2 * i) * KB) for i in range(2)]
        rS = [at(f"rS{i}", [P, S], F32, N0 + (44 + 2 * i) * KB) for i in range(2)]
        rcen = at("rcen", [P, S], F32, ARENA + 80 * KB)
        ro = at("ro", [P, RH, S], F32, ARENA + 82 * KB)
        r_hi = at("r_hi", [P, KD, S], F32R, N0)
        r_lo = at("r_lo", [P, KD, S], F32R, N0 + 16 * KB)
        rout = at("rout", [P, S], F32, N0 + 36 * KB)
        rsil = [at(f"rsil{i}", [P, S], F32, N0 + (32 + 2 * i) * KB) for i in range(2)]
        mixed = at("mixed", [P, KD, S], F32, ARENA + 82 * KB)
        sg = [at(f"sg{i}", [P, S], F32, N0 + (32 + 2 * i) * KB) for i in range(2)]
        mt = at("mt", [P, S], F32, N0 + 36 * KB)
        ang = [at(f"ang{i}", [P, S], F32, ARENA + (50 + 2 * i) * KB) for i in range(4)]
        posi = at("posi", [P, S], I32, ARENA + 58 * KB)
        poci = at("poci", [P, NT], I32, ARENA + 76 * KB)
        rbt = at("rbt", [32, 4], F32, ARENA + 76 * KB + 64)
        sc_f = at("sc_f", [P, KD], F32, ARENA + 97 * KB)
        lamt = at("lamt", [P, 8], F32, ARENA + 76 * KB + 192)
        step = [at(f"step{i}", [P, S], F32R, ARENA + (60 + 2 * i) * KB) for i in range(4)]
        bout = [at(f"bout{i}", [P, S], F32, ARENA + (68 + 2 * i) * KB) for i in range(2)]
        thr = at("thr", [P, P], F32, ARENA + 72 * KB)
        dcol = at("dcol", [P, 4], F32, ARENA + 72 * KB + 512)
        wf = at("wf", [P, 240], F32, ARENA + 73 * KB)
        win_hi = at("win_hi", [P, 240], F32R, ARENA + 74 * KB)
        win_lo = at("win_lo", [P, 240], F32R, ARENA + 75 * KB)
        cosM, sinM = cst[:, C_COSN:C_COSN + S], cst[:, C_SINN:C_SINN + S]
        posb, pen = cst[:, C_COSR:C_COSR + S], cst[:, C_SINR:C_SINR + S]
        lim = col[:, G_MISC:G_MISC + NT]
        neglam = col[:, G_LAM:G_LAM + 1]
        dq = at("dq", [P, 4, S], F32, ARENA)
        dk = at("dk", [P, 4, S], F32, ARENA + 8 * KB)
        dkz = at("dkz", [P, 8, S], F32, ARENA + 16 * KB)
        dv = at("dv", [P, NT, 512], F32, ARENA + 32 * KB)
        cqt = at("cqt", [P, 2, S], F32, ARENA + 40 * KB)
        ckr = at("ckr", [P, 2, S], F32, ARENA + 44 * KB)
        c_hi = at("c_hi", [P, 3, S], F32R, ARENA + 48 * KB)
        c_lo = at("c_lo", [P, 3, S], F32R, ARENA + 54 * KB)
        qm = at("qm", [P, 6, S], F32, ARENA + 60 * KB)
        kn = at("kn", [P, 4, S], F32, ARENA + 72 * KB)
        vm = at("vm", [P, NT, 512], F32, ARENA + 8 * KB)
        kpz = at("kpz", [P, 4, S], F32, ARENA + 48 * KB)
        hidden = [pen, PTm[0][:, 1, :], PTm[1][:, 1, :], posb]
        bias = at("bias", [P, NT, S], F32, ARENA + 40 * KB)
        latent2 = at("latent2", [P, 2, S], F32, ARENA + 56 * KB)
        latent_out = [cosM, sinM, latent2[:, 0, :], latent2[:, 1, :]]
        diff = at("diff", [P, 4, S], F32, ARENA + 72 * KB)
        diff_out = [diff[:, i, :] for i in range(4)]
        gate_out = [at(f"gate_out{i}", [P, S], F32, ARENA + (80 + 2 * i) * KB) for i in range(2)]
        z_hi = at("z_hi", [P, KD, S], F32R, ARENA + 16 * KB)
        z_lo = at("z_lo", [P, KD, S], F32R, ARENA + 32 * KB)
        osb = at("osb", [P, NT, D], F32, ARENA + 60 * KB)
        bias_dram = nc.dram_tensor("bias_scratch", [4, S, S], F32, kind="Internal").ap()
        bank = [ctx.enter_context(nc.psum_tensor(f"bank{i}", [P, S], F32)) for i in range(8)]

        ident = cst[:, C_ID:C_ID + P]
        ones = cst[:, C_ONE:C_ONE + P]

        slabs = []
        first_slab, first_acc = {}, {}
        n_acc = [0]

        def rows(w):
            return w.rearrange("(k p) n -> p k n", p=P)

        def stage(name, items, accs):
            first_slab[name] = len(slabs)
            first_acc[name] = n_acc[0]
            slabs.extend(items)
            n_acc[0] += accs

        def cols_slab(w, *spans, kt=KD):
            parts, c = [], 0
            for c0, c1 in spans:
                parts.append((0, kt, c, c + c1 - c0, w[:, :, c0:c1]))
                c += c1 - c0
            return (parts, kt, c)

        def ffn_slabs(f):
            wg, wu = rows(A[f + "_w_gate"][0]), rows(A[f + "_w_up"][0])
            wd = rows(A[f + "_w_down"][0])
            for half in range(2):
                items = []
                for m in range(half * HALF_F, (half + 1) * HALF_F):
                    items.append(([(0, 8, 0, P, wg[:, :, m * P:(m + 1) * P]),
                                   (8, 16, 0, P, wu[:, :, m * P:(m + 1) * P])], 16, P))
                stage(f"{f}_up{half}", items, 2 * HALF_F)
                items = [([(0, HALF_F, 0, P, wd[:, half * HALF_F:(half + 1) * HALF_F, m * P:(m + 1) * P])], HALF_F, P)
                         for m in range(KD)]
                stage(f"{f}_down{half}", items, KD)

        stage("xT", [], KD)
        ffn_slabs("ffn1")
        wi = rows(A["w_in"][0])
        stage("qk", [cols_slab(wi, (c, c + 256)) for c in range(0, W_KS, 256)]
              + [cols_slab(wi, (W_KS, W_VS), (W_KW, W_VW))], 12)
        stage("vg", [cols_slab(wi, (W_VS, W_KW), (W_VW, W_G)), cols_slab(wi, (W_G, W_RQ))], 8)
        stage("rqk", [cols_slab(wi, (c, c + 256)) for c in range(W_RQ, W_RV, 256)], 8)
        stage("rv", [cols_slab(wi, (c, c + 256)) for c in range(W_RV, W_RG, 256)], 16)
        stage("rg", [cols_slab(wi, (c, c + 256)) for c in range(W_RG, W_GM, 256)], 8)
        wna, wnr = rows(A["w_branch_nsa"][0]), rows(A["w_branch_ret"][0])
        items = []
        for m in range(KD):
            items.append(([(0, 8, 0, P, wi[:, :, W_GM + m * P:W_GM + (m + 1) * P]),
                           (8, 16, 0, P, wna[:, :, m * P:(m + 1) * P])], 16, P))
            items.append(([(0, 8, 0, P, wi[:, :, W_GM + D + m * P:W_GM + D + (m + 1) * P]),
                           (8, 16, 0, P, wnr[:, :, m * P:(m + 1) * P])], 16, P))
        stage("merge", items, 32)
        stage("wout", [cols_slab(rows(A["w_out"][0]), (c, c + 256)) for c in range(0, D, 256)], 8)
        ffn_slabs("ffn2")
        wa, wz = rows(A["ada_w_2"][0]), rows(A["w_in_2"][0])
        stage("cq", [cols_slab(wz, (Z_CQ, Z_CKV)), cols_slab(wz, (Z_CKV, Z_KR), (Z_KR, Z_G), (Z_KR, Z_G))], 4)
        stage("dqk", [cols_slab(wz, (c, c + 256)) for c in range(Z_DQ, Z_DV, 256)], 8)
        wuq = A["w_uq_2"][0].rearrange("(k p) (h e) -> p k h e", p=P, h=4)
        stage("uq", [([(k, k + 1, 0, 512, wuq[:, k, :, 0:128]) for k in range(2)]
                      + [(k, k + 1, 512, 768, wuq[:, k, :, 128:192]) for k in range(2)], 2, 768)], 6)
        stage("ukv", [([(0, 1, 0, 512, rows(A["w_uk_2"][0])), (1, 2, 0, 512, rows(A["w_uv_2"][0]))], 2, 512)], 8)
        stage("dv", [cols_slab(wz, (c, c + 256)) for c in range(Z_DV, Z_CQ, 256)], 8)
        stage("zg", [cols_slab(wz, (c, c + 256)) for c in range(Z_G, Z_G + D, 256)], 8)
        stage("wout2", [cols_slab(rows(A["w_out_2"][0]), (c, c + 256)) for c in range(0, D, 256)], 8)
        stage("outT", [], 8)
        names_in_order = list(first_slab)
        acc_after = []
        for i, name in enumerate(names_in_order):
            s1 = first_slab[names_in_order[i + 1]] if i + 1 < len(names_in_order) else len(slabs)
            a1 = first_acc[names_in_order[i + 1]] if i + 1 < len(names_in_order) else n_acc[0]
            ns = s1 - first_slab[name]
            acc_after += [first_acc[name] + (a1 - first_acc[name]) // ns * (j + 1) for j in range(ns)]
        landed, per_slot = [], [0, 0]
        for s, (parts, kt, w) in enumerate(slabs):
            per_slot[s % 2] += 16 * len(parts)
            landed.append(per_slot[s % 2])

        def slab_view(buf, s):
            _, kt, w = slabs[s]
            return buf[:, 0:kt * w].rearrange("p (k w) -> p k w", k=kt)

        s_raw = [sem(f"w_landed{i}") for i in range(2)]
        s_hi, s_lo, s_used = sem("w_hi_ready"), sem("w_lo_ready"), sem("w_used")
        acc_full, acc_free = sem("acc_full"), sem("acc_free")

        block = ctx.enter_context(nc.Block())


        @block.sync
        def _(sp):
            def load(dst, src, name):
                sp.dma_start(dst, src).then_inc(sem(name), 16)

            load(cst[:, 0:2 * P], A["consts"][:, 0:2 * P], "ident_landed")
            for t in range(NT):
                load(xin[:, t, :], A["x"][0, t * P:(t + 1) * P, :], f"xin_landed{t}")

            for s, (parts, kt, w) in enumerate(slabs):
                if s == 2:
                    load(cst[:, 2 * P:], A["consts"][:, 2 * P:], "const_landed")
                if s >= 2:
                    sp.wait_ge(s_hi, s - 1)
                    sp.wait_ge(s_lo, s - 1)
                v = slab_view(w_raw[s % 2], s)
                for k0, k1, c0, c1, src in parts:
                    dst = v[:, k0:k1, c0:c1]
                    if len(src.shape) == 3 and src.shape[1] == 4 and k1 - k0 == 1:
                        dst = v[:, k0, c0:c1].rearrange("p (h e) -> p h e", h=4)
                    sp.dma_start(dst, src).then_inc(s_raw[s % 2], 16)
                if 3 <= s < 19:
                    i = s - 3
                    if i >= 3:
                        sp.wait_ge(sem("ada_used"), i - 2)
                    load(ada_w[i % 3][:, :], wa[:, i // 2, 1536 * (i % 2):1536 * (i % 2) + 1536], f"ada_landed{i % 3}")
                if s == first_slab["qk"] + 1:
                    sp.wait_ge(acc_full, first_acc["qk"])
                    load(w1[:, :, :], A["cmp_k_w1"][0].rearrange("(c p) n -> p c n", p=P), "cmp_landed")
                    for i, n2 in enumerate(("cmp_k_w2", "cmp_v_w2")):
                        for dup in range(2):
                            load(w2[:, i, :, 64 * dup:64 * dup + 64], A[n2][0].rearrange("(c p) n -> p c n", p=P), "cmp_landed")
                    sp.wait_ge(sem("h_ready"), 2 * KD)
                    load(w1v[:, :, :], A["cmp_v_w1"][0].rearrange("(c p) n -> p c n", p=P)[:, 0:8, :], "cmp_landed")
                    load(pos_tok[:, :], A["cmp_pos_emb"][0].rearrange("(c j) d -> c (j d)", j=2), "cmp_landed")
                if s == first_slab["zg"] + 1:
                    for i in range(2):
                        sp.wait_ge(sem(f"bias_stored{i}"), 128)
                    for h in range(4):
                        for t in range(NT):
                            if h:
                                sp.wait_ge(sem("nm_ready"), 80 + 4 * h - 3 + t)
                            else:
                                sp.wait_ge(sem("kpe_ready"), 4)
                            load(bias[:, t, :], bias_dram[h, t * P:(t + 1) * P, :], f"bias_landed{t}")
                if s == first_slab["rqk"]:
                    sp.wait_ge(sem("cmp_k_half"), 1)
                    load(w1[:, 0:8, :], A["cmp_v_w1"][0].rearrange("(c p) n -> p c n", p=P)[:, 8:16, :], "cmp_v_landed")
                if s == first_slab["rv"] + 3:
                    for h in range(RH):
                        if h < 2:
                            sp.wait_ge(sem("o_free"), 8)
                        else:
                            sp.wait_ge(sem("r_m"), 4 * (h - 1))
                        load(dec[h % 2][:, :], A["decay"][h], f"dec_landed{h % 2}")
                if s == first_slab["ffn2_up0"] + 1:
                    sp.wait_ge(acc_full, first_acc["wout"])
                    load(posi[:, :], A["positions_2"][0:1, :].broadcast_to([P, S]), "pos_landed")
                    load(poci[:, :], A["positions_2"][0].rearrange("(t p) -> p t", p=P), "pos_landed")
                    load(rbt[:, :], A["rel_bias_2"], "pos_landed")
            for t in range(NT):
                sp.wait_ge(acc_free, first_acc["outT"] + 2 * t + 2)
                sp.dma_start(out[0, t * P:(t + 1) * P, :], osb[:, t, :]).then_inc(sem("out_stored"), 16)
            sp.wait_ge(sem("out_stored"), 16 * NT)

        N_COL_DMAS = 12 + 1 + 8 + 1

        @block.gpsimd
        def _(pool):
            for s in range(len(slabs)):
                if s == first_slab["zg"] + 1:
                    pool.wait_ge(sem("hidden_ready"), 1)
                    for i in range(16):
                        t = i % 4
                        pool.wait_ge(sem(f"bias_landed{t}"), 16 * (i // 4 + 1))
                        pool.tensor_add(bias[:, t, :], bias[:, t, :], hidden[t]).then_inc(sem("bias_ready"), 1)
                pool.wait_ge(s_hi, s + 1)
                n = slabs[s][1] * slabs[s][2]
                pool.tensor_sub(w_lo[s % 2][:, 0:n], w_raw[s % 2][:, 0:n], w_hi[s % 2][:, 0:n]).then_inc(s_lo, 1)

        count = {}

        def tick(ins, name):
            ins.then_inc(sem(name), 1)
            count[name] = count.get(name, 0) + 1
            return count[name]

        BIG_NORMS = 5

        UNITS = [(hp, t, e) for hp in range(8) for t in range(NT) for e in range(2)]
        UNITS2 = [(kind, h, t) for kind in (1, 0) for h in range(4) for t in range(NT)]

        cq0, dq0, uq0, ukv0 = (first_acc[n] for n in ("cq", "dqk", "uq", "ukv"))
        NORMS2 = [([(cqt[:, k, :], ("acc_free", cq0 + k + 1), C_ONE) for k in range(2)], 256),
                  ([(ckr[:, 0, :], ("acc_free", cq0 + 3), C_ONE)], 128)]
        for j in range(8):
            NORMS2.append(([((dq, dk)[j // 4][:, j % 4, :], ("acc_free", dq0 + j + 1), C_BLK)], 64))
        for h in range(4):
            NORMS2.append(([(qm[:, h, :], ("acc_free", uq0 + h + 1), C_ONE),
                            (qm[:, 4 + h // 2, :], ("rope_done", 20 + h // 2 + 1), C_HALF + P * (h % 2))], 192))
        for h in range(4):
            NORMS2.append(([(kn[:, h, :], ("acc_free", ukv0 + h + 1), C_ONE),
                            (ckr[:, 1, :], ("rope_done", 20), C_HALF)], 192))
        for h in range(4):
            NORMS2.append(([(diff_out[h], ("o_free", 12 + h + 1), C_ONE)], 128))
        NORM_SLOT = {5: [0], 6: [1], **{7 + m: [2 + m] for m in range(8)}, **{20 + 2 * h: [10 + h] for h in range(4)},
                     **{27 + h: [14 + h] for h in range(4)}}
        BIAS_SLOTS = 12
        bias_groups = lambda i: range(P * i // BIAS_SLOTS, P * (i + 1) // BIAS_SLOTS) if i < BIAS_SLOTS else range(0)

        rope_bank = lambda j: bank[4 + j % 2] if j < 19 else bank[4]

        @block.scalar
        def _(act):
            slab_at = [0]

            def split_next():
                s = slab_at[0]
                if s >= len(slabs):
                    return
                slab_at[0] += 1
                act.wait_ge(s_raw[s % 2], landed[s])
                if s >= 2:
                    act.wait_ge(acc_full, acc_after[s - 2])
                n = slabs[s][1] * slabs[s][2]
                act.activation(w_hi[s % 2][:, 0:n], w_raw[s % 2][:, 0:n], ACT.Copy).then_inc(s_hi, 1)

            def each_slab(name, tile_work, per_slab):
                a = first_acc[name]
                i = names_in_order.index(name)
                n = first_slab[names_in_order[i + 1]] - first_slab[name]
                for s in range(n):
                    split_next()
                    for j in range(per_slab):
                        tile_work(s * per_slab + j, a + s * per_slab + j)

            nothing = lambda i, a: None

            def square(n, k):
                act.wait_ge(acc_free, first_acc[("xT", "ffn1_down1", "wout", "ffn2_down1")[n]] + k + 1)
                if 7 * n + k:
                    act.wait_ge(sem("sq_added"), 7 * n + (max(1, k - 2) if k > 1 else 0))
                act.activation(sq[k % 2][:, :], x[:, k, :], ACT.Square).then_inc(sem("nsq"), 1)
                if n == 3:
                    if k > 1:
                        act.wait_ge(sem("sqg_added"), max(1, k - 2))
                    act.activation(sqg[k % 2][:, :], x[:, k, :], ACT.Square, scale=col[:, G_FIN + k:G_FIN + k + 1]).then_inc(sem("nsqg"), 1)

            def square_before(n):
                return lambda i, a: square(n, i - 1) if i else None

            def big_norm(n, first=KD - 1):
                for k in range(first, KD):
                    square(n, k)
                act.wait_ge(sem("nmm"), n + 1)
                if n:
                    act.wait_ge(sem("rs_ready"), n)
                act.activation(std[:, :], bank[5][:, :], ACT.Sqrt, bias=col[:, G_EPS:G_EPS + 1], scale=1.0 / D).then_inc(sem("nstd"), 1)

            def split_h(n):
                for k in range(KD):
                    act.wait_ge(sem("hn_ready"), n * KD + k + 1)
                    act.activation(h_hi[:, k, :], (tmp, tmp2)[k % 2][:, :], ACT.Copy).then_inc(sem("h_hi_ready"), 1)

            def squares2(j):
                if j in (11, 13):
                    act.wait_ge(sem("qpe_ready"), j - 10)
                for src, ready, _ in NORMS2[j][0]:
                    act.wait_ge(sem(ready[0]), ready[1])
                    q = count.get("ssq", 0)
                    if q >= 2:
                        act.wait_ge(sem("smm"), q - 1)
                    tick(act.activation(sq[q % 2][:, :], src, ACT.Square), "ssq")

            def deviation2(j):
                n = sum(len(NORMS2[i][0]) for i in range(j + 1))
                act.wait_ge(sem("smm"), n)
                act.wait_ge(sem("rs_ready"), BIG_NORMS + j)
                tick(act.activation(std[:, :], bank[5][:, :], ACT.Sqrt, bias=col[:, G_EPS:G_EPS + 1], scale=1.0 / NORMS2[j][1]), "sstd")

            def act_load(dst, src):
                act.dma_start(dst, src).then_inc(sem("col_landed"), 16)

            vec = [(G_F1, A["ffn1_norm"][0]), (G_MIX, A["mix_norm"][0]), (G_F2, A["ffn2_norm"][0]), (G_FIN, A["final_norm"]),
                   (G_N2, A["norm_g_2"][0]), (G_C, A["c_2"][0]), (G_ADAB, A["ada_b_2"][0]), (G_QA, A["mla_q_a_norm_2"][0]),
                   (G_KVA, A["mla_kv_a_norm_2"][0]), (G_SUB, A["diff_sub_norm_2"][0]),
                   (G_QN, A["mla_q_norm_2"][0, 0:128]), (G_KN, A["mla_k_norm_2"][0, 0:128])]
            for g, v in vec:
                k = v.shape[0] // P
                act_load(col[:, g:g + k], v.rearrange("(k p) -> p k", p=P))
            act_load(col[:, G_GN:G_GN + RH], A["ret_gn_gain"][0].rearrange("h e -> e h"))
            for r0 in (0, 64):
                for g, v in ((G_DQ, A["diff_q_norm_2"][0]), (G_DK, A["diff_k_norm_2"][0]),
                             (G_QP, A["mla_q_norm_2"][0, 128:192]), (G_KP, A["mla_k_norm_2"][0, 128:192])):
                    act_load(col[r0:r0 + 64, g:g + 1], v.rearrange("(p k) -> p k", k=1))
            act_load(col[0:64, G_LAM:G_LAM + 4], A["diff_lambda_2"][0].rearrange("a e -> e a"))

            act.wait_ge(sem("eps_set"), 2)
            for k in range(KD - 1):
                square(0, k)
            split_next()
            big_norm(0)
            split_h(0)
            act.wait_ge(sem("col_landed"), 16 * N_COL_DMAS)
            act.activation(sc_f[:, :], col[:, G_C:G_C + KD], ACT.Silu).then_inc(sem("c_silu"), 1)

            def ffn(f, n):
                def gate(i, a):
                    if f == "ffn2" and a < first_acc["ffn2_down0"]:
                        prepare(i)
                    if i % 2 == 0:
                        m = count.get("act_gate", 0)
                        act.wait_ge(acc_full, a + 1)
                        if m >= 2:
                            act.wait_ge(sem("hid_ready"), m - 1)
                        tick(act.activation(silu[m % 2][:, :], bank[a % 4][:, :], ACT.Silu), "act_gate")
                for half in range(2):
                    each_slab(f"{f}_up{half}", gate, 2)
                    each_slab(f"{f}_down{half}", square_before(n) if half else nothing, 1)

            def prepare(i):
                if i == 7:
                    act.wait_ge(sem("lam_sum"), 1)
                    act.activation(lamt[:, 2:4], bank[7][:, 0:2], ACT.Exp).then_inc(sem("lam_exp"), 1)
                if i == 15:
                    act.wait_ge(sem("ang_ready"), 1)
                    act.activation(sinM, ang[0][:, :], ACT.Sin)
                    act.activation(cosM, ang[1][:, :], ACT.Sin).then_inc(sem("trig_ready"), 1)

            ffn("ffn1", 1)
            big_norm(1)
            split_h(1)
            each_slab("qk", nothing, 2)

            def vg(i, a):
                if i >= 4:
                    act.wait_ge(acc_full, a + 1)
                    act.activation(gates[:, i - 4, :], bank[a % 4][:, 0:48], ACT.Sigmoid).then_inc(sem("gates_ready"), 1)
            each_slab("vg", vg, 4)
            for i in range(2):
                act.wait_ge(sem("gelu_in"), i + 1)
                act.activation(gl[1][:, :], gl[0][:, :], ACT.Tanh, scale=0.7978845608028654).then_inc(sem("gelu_tanh"), 1)
            for t in range(NT):
                act.wait_ge(sem("cmp_in"), t + 1)
                act.activation(sc[:, :, :], sc[:, :, :], ACT.Exp, scale=SCALE).then_inc(sem("cmp_exp"), 1)

            def exps(u, b, n, maps, scale):
                act.wait_ge(sem("nm_ready"), u + 1)
                if u >= 2:
                    act.wait_ge(sem("pt_full"), u - 1)
                for i in range(maps):
                    last = act.activation(Pm[u % 2][:, i, 0:n], bank[2 * (u % 2) + i][:, 0:n], ACT.Exp,
                                          bias=mstat[:, u % 2, 2 + i:3 + i], scale=scale,
                                          accum_out=mstat[:, u % 2, 4 + i:5 + i])
                last.then_inc(sem("p_exp"), 1)

            def evac(u, n, maps):
                act.wait_ge(sem("pt_full"), u + 1)
                if u >= 2:
                    act.wait_ge(sem("pv_done"), u - 1)
                for i in range(maps):
                    last = act.activation(PTm[u % 2][:, i, 0:n], bank[4 + i][:, 0:n], ACT.Copy)
                last.then_inc(sem("pt_evac"), 1)

            exps(0, 0, P, 2, SCALE)
            for u in range(len(UNITS)):
                if u + 1 < len(UNITS):
                    exps(u + 1, 0, (UNITS[u + 1][1] + 1) * P, 2, SCALE)
                evac(u, (UNITS[u][1] + 1) * P, 2)
            each_slab("rqk", nothing, 2)
            each_slab("rv", nothing, 4)
            def rg(i, a):
                if i < RH:
                    act.wait_ge(sem("ln_c"), i + 1)
                    if i >= 2:
                        act.wait_ge(sem("ln2"), i - 1)
                    act.activation(rS[i % 2][:, :], ro[:, i, :], ACT.Square).then_inc(sem("ln_s"), 1)
                if i >= 1:
                    act.wait_ge(sem("ln2"), i)
                    if i >= 2:
                        act.wait_ge(sem("ln_r"), i - 1)
                    act.activation(rcen[:, :], bank[5][:, :], ACT.Sqrt, bias=col[:, G_GNEPS:G_GNEPS + 1], scale=1.0 / P).then_inc(sem("ln_t"), 1)
                    act.wait_ge(acc_full, a)
                    if i >= 3:
                        act.wait_ge(acc_free, a - 2)
                    act.activation(rsil[(i - 1) % 2][:, :], bank[(a - 1) % 4][:, :], ACT.Silu).then_inc(sem("rg_ready"), 1)
            each_slab("rg", rg, 2)
            rg(RH, first_acc["merge"])

            def merge(i, a):
                if i % 2 == 0:
                    j = i // 2
                    act.wait_ge(acc_full, a + 1)
                    act.wait_ge(acc_free, a - 2 if j >= 2 else first_acc["merge"])
                    act.activation(sg[j % 2][:, :], bank[a % 4][:, :], ACT.Sigmoid).then_inc(sem("sg_ready"), 1)
            each_slab("merge", merge, 2)
            each_slab("wout", square_before(2), 2)
            big_norm(2)
            split_h(2)
            ffn("ffn2", 3)
            big_norm(3)
            act.wait_ge(sem("gsum_ready"), 1)
            act.activation(std[:, :], tmp[:, :], ACT.Sqrt, bias=col[:, G_EPS:G_EPS + 1], scale=1.0 / D).then_inc(sem("nstd"), 1)
            split_h(3)

            def store_bias(i):
                act.wait_ge(sem("bias_out"), i + 1)
                act.dma_start(bias_dram[:, 32 * i:32 * i + 32, :].rearrange("h q k -> q h k"), bout[i % 2][:, :]).then_inc(sem(f"bias_stored{i % 2}"), 16)

            def beside(slot0):
                def work(i, a):
                    slot = slot0 + i
                    groups = bias_groups(slot - 1) if slot else range(0)
                    for b in groups:
                        if b % 8 == 7:
                            t = b // 8
                            act.wait_ge(sem("bmm"), b + 1)
                            if t >= 2:
                                act.wait_ge(sem(f"bias_stored{t % 2}"), 16 * (t // 2))
                            act.activation(bout[t % 2][:, :], bank[6 + t % 2][:, :], ACT.Copy).then_inc(sem("bias_out"), 1)
                            store_bias(t)
                    for j in NORM_SLOT.get(slot, []):
                        deviation2(j)
                    for j in NORM_SLOT.get(slot + 1, []):
                        squares2(j)
                return work
            for name, per, slot0 in (("cq", 2, 0), ("dqk", 2, 4), ("uq", 6, 12), ("ukv", 8, 18), ("dv", 4, 26)):
                each_slab(name, beside(slot0), per)
            exps(64, 0, S, 1, 1.0)
            for v in range(len(UNITS2)):
                if v + 1 < len(UNITS2):
                    exps(65 + v, 0, S, 2 - UNITS2[v + 1][0], 1.0)
                evac(64 + v, S, 1)
            squares2(18)

            def zg(i, a):
                act.wait_ge(acc_full, a + 1)
                if i >= 2:
                    act.wait_ge(acc_free, a - 1)
                act.activation(gate_out[i % 2][:, :], bank[a % 4][:, :], ACT.Silu).then_inc(sem("zg_ready"), 1)
                if i < 4:
                    deviation2(18 + i)
                if i < 3:
                    squares2(19 + i)
            each_slab("zg", zg, 2)
            each_slab("wout2", nothing, 2)

        @block.tensor
        def _(pe):
            slab_at, acc_at = [0], [0]

            def use_slab():
                s = slab_at[0]
                slab_at[0] += 1
                pe.wait_ge(s_lo, s + 1)
                return slab_view(w_hi[s % 2], s), slab_view(w_lo[s % 2], s)

            def open_acc():
                a = acc_at[0]
                if a >= 4:
                    pe.wait_ge(acc_free, a - 3)
                return bank[a % 4]

            def close_acc(ins):
                ins.then_inc(acc_full, 1)
                acc_at[0] += 1

            def mm3(o, l, r, first, last):
                pe.matmul(o, l[0], r[0], start=first, stop=False)
                pe.matmul(o, l[0], r[1], start=False, stop=False)
                return pe.matmul(o, l[1], r[0], start=False, stop=last)

            def feature_tile(wh, wl, k0, kt, cols, src, width=P, ready=None):
                o = open_acc()
                for k in range(kt):
                    if ready:
                        pe.wait_ge(sem(ready[0]), ready[1] + k + 1)
                    ins = mm3(o[0:width, :], (wh[:, k0 + k, cols], wl[:, k0 + k, cols]), (src[0][:, k, :], src[1][:, k, :]),
                              k == 0, k == kt - 1)
                close_acc(ins)

            def first_tiles(wh, wl, places, src, ready):
                o = [open_acc()]
                a = acc_at[0] + 1
                pe.wait_ge(acc_free, a - 3)
                o.append(bank[a % 4])
                for k in range(KD):
                    pe.wait_ge(sem(ready[0]), ready[1] + k + 1)
                    for i, (k0, cols) in enumerate(places):
                        ins = mm3(o[i][:, :], (wh[:, k0 + k, cols], wl[:, k0 + k, cols]), (src[0][:, k, :], src[1][:, k, :]),
                                  k == 0, k == KD - 1)
                        if k == KD - 1:
                            close_acc(ins)

            def token_tile(wh, wl, kt, src, t, n, k0=0):
                o = open_acc()
                for k in range(kt):
                    ins = mm3(o[:, 0:n], (src[0][:, k, t * P:(t + 1) * P], src[1][:, k, t * P:(t + 1) * P]),
                              (wh[:, k0 + k, 0:n], wl[:, k0 + k, 0:n]), k == 0, k == kt - 1)
                close_acc(ins)

            def big_norm(n):
                pe.wait_ge(sem("sq_sum"), n + 1)
                if n:
                    pe.wait_ge(sem("nstd"), n)
                pe.matmul(bank[5][:, :], ones, sqsum[:, :], start=True, stop=True).then_inc(sem("nmm"), 1)
                if n == 3:
                    pe.matmul(bank[6][:, :], ones, sqgsum[:, :], start=True, stop=True).then_inc(sem("gmm"), 1)

            def small_norm(j):
                srcs, _ = NORMS2[j]
                if j:
                    pe.wait_ge(sem("sstd"), j)
                for i, (_, _, mat) in enumerate(srcs):
                    q = count.get("smm", 0)
                    pe.wait_ge(sem("ssq"), q + 1)
                    tick(pe.matmul(bank[5][:, :], cst[:, mat:mat + P], sq[q % 2][:, :], start=i == 0, stop=i == len(srcs) - 1), "smm")

            def rotate(src, which, n=S):
                j = count.get("rope_mm", 0)
                if j >= 2:
                    pe.wait_ge(sem("rope_done"), j - 1 if j < 19 else j)
                tick(pe.matmul(rope_bank(j)[:, 0:n], cst[:, which:which + P], src, start=True, stop=True), "rope_mm")

            pe.wait_ge(sem("ident_landed"), 16)
            for k in range(KD):
                o = open_acc()
                for t in range(NT):
                    if k == 0:
                        pe.wait_ge(sem(f"xin_landed{t}"), 16)
                    ins = pe.transpose(o[:, t * P:(t + 1) * P], xin[:, t, k * P:(k + 1) * P], ident)
                close_acc(ins)
            big_norm(0)

            def ffn(f, n):
                for half in range(2):
                    for m in range(HALF_F):
                        wh, wl = use_slab()
                        if f == "ffn2" and half == 0 and m == 3:
                            pe.wait_ge(sem("lam_prod"), 1)
                            pe.matmul(bank[7][:, 0:2], ones, lamt[:, 0:2], start=True, stop=True).then_inc(sem("lam_sum"), 1)
                            pe.wait_ge(sem("pos_landed"), 48)
                            pe.wait_ge(sem("ln_c"), RH)
                            pe.matmul(bank[4][:, 0:4], cst[0:32, C_PERM:C_PERM + P], rbt[:, :], start=True, stop=True).then_inc(sem("dcol_full"), 1)
                        if half == 0 and m == 0:
                            first_tiles(wh, wl, ((0, slice(0, P)), (KD, slice(0, P))), (h_hi, h_lo), ("h_ready", 8 * n))
                            continue
                        feature_tile(wh, wl, 0, KD, slice(0, P), (h_hi, h_lo))
                        feature_tile(wh, wl, KD, KD, slice(0, P), (h_hi, h_lo))
                    if f == "ffn1" and half:
                        pe.wait_ge(sem("ada_used"), 16)
                        for j in range(24):
                            ins = pe.matmul(bank[7][:, j:j + 1], ada_sum[:, j * P:(j + 1) * P], ones[:, 0:1], start=True, stop=True)
                        ins.then_inc(sem("ada_full"), 1)
                    for m in range(KD):
                        wh, wl = use_slab()
                        hid0 = (0 if f == "ffn1" else KF) + half * HALF_F
                        feature_tile(wh, wl, 0, HALF_F, slice(0, P), (u_hi, u_lo), ready=("hid_ready", hid0) if m == 0 else None)

            ffn("ffn1", 0)
            pe.wait_ge(sem("const_landed"), 16)
            big_norm(1)
            for i in range(6):
                wh, wl = use_slab()
                if i == 0:
                    first_tiles(wh, wl, ((0, slice(0, P)), (0, slice(P, 2 * P))), (h_hi, h_lo), ("h_ready", 8))
                    pe.wait_ge(acc_free, first_acc["qk"] + 1)
                    rotate(qT[:, 0, :], C_ROTN)
                    continue
                for j in range(2):
                    feature_tile(wh, wl, 0, KD, slice(j * P, (j + 1) * P), (h_hi, h_lo))
                    m = 2 * i + j - 1
                    if m < 8:
                        pe.wait_ge(acc_free, first_acc["qk"] + m + 1)
                        rotate(qT[:, m, :], C_ROTN)
                    elif m == 10:
                        pe.wait_ge(acc_free, first_acc["qk"] + m + 1)
                        rotate(kv_s[:, 0, :], C_ROTN)
            wh, wl = use_slab()
            for t in range(NT):
                token_tile(wh, wl, KD, (h_hi, h_lo), t, 256)
                if t == 0:
                    pe.wait_ge(acc_free, first_acc["qk"] + 12)
                    rotate(kv_s[:, 1, :], C_ROTN)
            wh, wl = use_slab()
            for t in range(NT):
                token_tile(wh, wl, KD, (h_hi, h_lo), t, 48)
            pe.wait_ge(sem("cmp_landed"), 16 * 7)
            pe.wait_ge(sem("rope_done"), 10)
            pe.transpose(bank[4][:, 0:16], pos_tok[:, :], ident[0:16, 0:16]).then_inc(sem("posT_full"), 1)
            pe.wait_ge(sem("posT_ready"), 1)
            pe.wait_ge(sem("T2_ready"), 8)
            pairs = [T2[:, i, :, :].rearrange("p g t -> p (g t)") for i in range(2)]
            for i in range(2):
                for c in range(16):
                    w = w1[:, c, :] if i == 0 else (w1v if c < 8 else w1)[:, c % 8, :]
                    if (i, c) == (1, 8):
                        pe.wait_ge(sem("cmp_v_landed"), 16)
                    pe.matmul(bank[6 + i][0:NROW, 0:256], pairs[i][:, 2 * c:2 * c + 16 * (NROW - 1) + 1:16], w, start=c == 0, stop=False)
                    ins = pe.matmul(bank[6 + i][0:NROW, 0:256], posT[:, c:c + 1].to_broadcast([P, NROW]), w, start=False, stop=c == 15)
                    if (i, c) == (0, 7):
                        ins.then_inc(sem("cmp_k_half"), 1)
                ins.then_inc(sem("cmp_hid"), 1)
            for i in range(2):
                pe.wait_ge(sem("hid_cmp_ready"), i + 1)
                for c in range(2):
                    ins = pe.transpose(bank[4][:, 64 * (2 * i + c):64 * (2 * i + c) + NROW], hid[:, i, c * P:(c + 1) * P], ident[0:NROW, 0:NROW])
            ins.then_inc(sem("hidT_full"), 1)
            pe.wait_ge(sem("hidT_ready"), 4)
            for c in range(2):
                pe.matmul(bank[5][:, 0:64], w2[:, 0, c, :], hidT[:, 0, c, :, :], start=c == 0, stop=c == 1)
            for g in range(GROUPS):
                for c in range(2):
                    ins = pe.matmul(bank[5][:, 128 + 64 * g:192 + 64 * g], hrep[:, c, g, :, :],
                                    w2[:, 1, c, 0:64], start=c == 0, stop=c == 1)
            ins.then_inc(sem("cmp_kv"), 1)
            pe.wait_ge(sem("kcr_ready"), 1)
            rotate(kcr[:, :, :], C_ROTN, 64)
            pe.wait_ge(sem("rope_done"), 11)
            for t in range(NT):
                if t >= 2:
                    pe.wait_ge(sem("cmp_in"), t - 1)
                for h in range(HEADS):
                    ins = pe.matmul(bank[6 + t % 2][:, h * NCP:(h + 1) * NCP], qT[:, h // 2, t * P:(t + 1) * P],
                                    kcz[:, h % 2, h // 8, :], start=True, stop=True)
                ins.then_inc(sem("cmp_s"), 1)
                pe.wait_ge(sem("cmp_p"), t + 1)
                if t >= 2:
                    pe.wait_ge(sem("cmp_pT"), t - 1)
                for j in range(4):
                    ins = pe.transpose(bank[4 + t % 2][:, j * P:(j + 1) * P], sc[:, 4 * j:4 * j + 4, :], ident)
                ins.then_inc(sem("cmp_t"), 1)

            def scores(u):
                hp, t, e = UNITS[u]
                n, g = (t + 1) * P, hp // 4
                if u >= 2:
                    pe.wait_ge(sem("p_exp"), u - 1)
                for i in range(2):
                    ins = pe.matmul(bank[2 * (u % 2) + i][:, 0:n], qT[:, hp, t * P:(t + 1) * P], kz[:, i, g, e, 0:n],
                                    start=True, stop=True)
                ins.then_inc(sem("s_full"), 1)

            def turn(u, blocks, maps):
                pe.wait_ge(sem("p_ready"), u + 1)
                if u:
                    pe.wait_ge(sem("pt_evac"), u)
                for i in range(maps):
                    for b in range(blocks):
                        ins = pe.transpose(bank[4 + i][:, b * P:(b + 1) * P], Pm[u % 2][:, i, b * P:(b + 1) * P], ident)
                ins.then_inc(sem("pt_full"), 1)

            def values(u):
                hp, t, e = UNITS[u]
                h, g, r = 2 * hp + e, hp // 4, 64 * e
                pe.wait_ge(sem("pt_evac"), u + 1)
                if (t, e) == (0, 0) and hp >= 2:
                    pe.wait_ge(sem("o_free"), hp - 1)
                o = bank[6 + hp % 2][r:r + 64, t * P:(t + 1) * P]
                pe.matmul(o, vcz[:, h % 4, g, :], pTc[:, t, h // 4, :], start=True, stop=False)
                for i in range(2):
                    for b in range(t + 1):
                        ins = pe.matmul(o, vtok[:, b, 128 * i + 64 * g:128 * i + 64 * g + 64], PTm[u % 2][:, i, b * P:(b + 1) * P],
                                        start=False, stop=i == 1 and b == t)
                ins.then_inc(sem("pv_done"), 1)

            pe.wait_ge(acc_free, first_acc["rqk"])
            pe.wait_ge(sem("cmp_pT"), NT)
            scores(0)
            scores(1)
            for u in range(len(UNITS)):
                if u + 2 < len(UNITS):
                    scores(u + 2)
                turn(u, UNITS[u][1] + 1, 2)
                if u:
                    values(u - 1)
            values(len(UNITS) - 1)
            for i in range(4):
                wh, wl = use_slab()
                for j in range(2):
                    feature_tile(wh, wl, 0, KD, slice(j * P, (j + 1) * P), (h_hi, h_lo))
                    m = 2 * i + j - 1
                    if m >= 0:
                        pe.wait_ge(acc_free, first_acc["rqk"] + m + 1)
                        rotate((rq, rk)[m // 4][:, m % 4, :], C_ROTR)
            for s in range(4):
                wh, wl = use_slab()
                for t in range(NT):
                    token_tile(wh, wl, KD, (h_hi, h_lo), t, 256)
                    if (s, t) == (0, 0):
                        pe.wait_ge(acc_free, first_acc["rqk"] + 8)
                        rotate(rk[:, 3, :], C_ROTR)
            pe.wait_ge(sem("rope_done"), 19)
            pe.wait_ge(acc_free, first_acc["rg"])

            def r_scores(i):
                h, kb = i // 4, i % 4
                if h:
                    pe.wait_ge(sem("r_m"), i - 3)
                pe.matmul(bank[kb][:, 0:S - kb * P], rkz[:, h, kb * P:(kb + 1) * P], rq[:, h // 2, kb * P:S],
                          start=True, stop=True).then_inc(sem("r_s"), 1)

            def r_values(i):
                h, kb = i // 4, i % 4
                pe.wait_ge(sem("r_m"), i + 1)
                if kb == 0 and h >= 2:
                    pe.wait_ge(sem("r_o"), h - 1)
                pe.matmul(bank[6 + h % 2][:, kb * P:S], rv[:, kb, h * P:(h + 1) * P], rS[kb % 2][:, 0:S - kb * P],
                          start=kb == 0, stop=kb == 3).then_inc(sem("r_pv"), 1)

            r_scores(0)
            for i in range(4 * RH):
                if i + 1 < 4 * RH:
                    r_scores(i + 1)
                r_values(i)
            pe.wait_ge(sem("r_m"), 4 * RH)
            for h in range(RH + 1):
                if h < RH:
                    pe.wait_ge(sem("r_o"), h + 1)
                    pe.wait_ge(sem("ln_c"), h)
                    pe.matmul(bank[4][:, :], ones, ro[:, h, :], start=True, stop=True).then_inc(sem("ln1"), 1)
                    if h % 2 == 0:
                        wh, wl = use_slab()
                    feature_tile(wh, wl, 0, KD, slice(h % 2 * P, h % 2 * P + P), (h_hi, h_lo))
                    pe.wait_ge(sem("ln_s"), h + 1)
                    pe.wait_ge(sem("ln_t"), h)
                    pe.matmul(bank[5][:, :], ones, rS[h % 2][:, :], start=True, stop=True).then_inc(sem("ln2"), 1)
            for m in range(KD):
                for i, src in enumerate(((a_hi, a_lo), (r_hi, r_lo))):
                    wh, wl = use_slab()
                    feature_tile(wh, wl, 0, KD, slice(0, P), (h_hi, h_lo))
                    if m == 0 and i == 1:
                        pe.wait_ge(sem("r_ready"), 8)
                    feature_tile(wh, wl, KD, KD, slice(0, P), src)
            for s in range(4):
                wh, wl = use_slab()
                if s == 0:
                    first_tiles(wh, wl, ((0, slice(0, P)), (0, slice(P, 2 * P))), (h_hi, h_lo), ("mh_ready", 0))
                    continue
                for j in range(2):
                    feature_tile(wh, wl, 0, KD, slice(j * P, (j + 1) * P), (h_hi, h_lo))
            pe.wait_ge(sem("ln_t"), RH)
            big_norm(2)
            ffn("ffn2", 2)
            big_norm(3)
            def bias_steps(i):
                t, g = i // 8, i % 8
                if i == 0:
                    pe.wait_ge(sem("win_ready"), 1)
                    pe.wait_ge(sem("lam_exp"), 1)
                pe.wait_ge(sem("step_ready"), i + 1)
                if g == 0 and t >= 2:
                    pe.wait_ge(sem("bias_out"), t - 1)
                w = slice(112 - 16 * g, 240 - 16 * g)
                pe.matmul(bank[6 + t % 2][:, :], win_hi[:, w], step[i % 4][:, :], start=g == 0, stop=False)
                pe.matmul(bank[6 + t % 2][:, :], win_lo[:, w], step[i % 4][:, :], start=False, stop=g == 7).then_inc(sem("bmm"), 1)

            slot_at = [0]

            def beside():
                slot = slot_at[0]
                slot_at[0] += 1
                for i in bias_groups(slot):
                    bias_steps(i)
                if slot == 4:
                    pe.wait_ge(sem("trig_ready"), 1)
                    pe.wait_ge(acc_free, cq0 + 4)
                    rotate(ckr[:, 1, :], C_ROTR)
                if slot in (18, 19):
                    pe.wait_ge(acc_free, uq0 + slot - 13)
                    rotate(qm[:, slot - 14, :], C_ROTR)
                for j in NORM_SLOT.get(slot, []):
                    small_norm(j)

            for s in range(2):
                wh, wl = use_slab()
                if s == 0:
                    first_tiles(wh, wl, ((0, slice(0, P)), (0, slice(P, 2 * P))), (h_hi, h_lo), ("h_ready", 24))
                    beside()
                    beside()
                    continue
                for j in range(2):
                    feature_tile(wh, wl, 0, KD, slice(j * P, (j + 1) * P), (h_hi, h_lo))
                    beside()
            for s in range(4):
                wh, wl = use_slab()
                for j in range(2):
                    feature_tile(wh, wl, 0, KD, slice(j * P, (j + 1) * P), (h_hi, h_lo))
                    beside()
            pe.wait_ge(sem("c_split"), 3)
            wh, wl = use_slab()
            for j in range(6):
                feature_tile(wh, wl, 0, 2, slice(j * P, (j + 1) * P), (c_hi, c_lo))
                beside()
            wh, wl = use_slab()
            cc = (c_hi[:, 2:3, :], c_lo[:, 2:3, :])
            for j in range(4):
                feature_tile(wh, wl, 0, 1, slice(j * P, (j + 1) * P), cc)
                beside()
            for t in range(NT):
                token_tile(wh, wl, 1, cc, t, 512, 1)
                beside()
            for s in range(2):
                wh, wl = use_slab()
                for t in range(NT):
                    token_tile(wh, wl, KD, (h_hi, h_lo), t, 256)
                    beside()

            def scores2(v):
                kind, h, t = UNITS2[v]
                u, q = 64 + v, slice(UNITS2[v][2] * P, UNITS2[v][2] * P + P)
                pe.wait_ge(sem("p_exp"), u - 1)
                b = 2 * (u % 2)
                if kind == 0:
                    for i in range(2):
                        ins = pe.matmul(bank[b + i][:, :], dq[:, h, q], dkz[:, 2 * h + i, :], start=True, stop=True)
                else:
                    pe.matmul(bank[b][:, :], qm[:, h, q], kn[:, h, :], start=True, stop=False)
                    ins = pe.matmul(bank[b][:, :], qm[:, 4 + h // 2, q], kpz[:, h, :], start=False, stop=True)
                ins.then_inc(sem("s_full"), 1)

            def values2(v):
                kind, h, t = UNITS2[v]
                u, i = 64 + v, v // 4
                pe.wait_ge(sem("pt_evac"), u + 1)
                if t == 0:
                    pe.wait_ge(sem("o_free"), 8 + i - 1)
                o = bank[6 + i % 2][:, t * P:(t + 1) * P]
                for b in range(NT):
                    ins = pe.matmul(o, (dv, vm)[kind][:, b, h * P:(h + 1) * P], PTm[u % 2][:, 0, b * P:(b + 1) * P], start=b == 0, stop=b == NT - 1)
                ins.then_inc(sem("pv_done"), 1)

            pe.wait_ge(sem("kpe_ready"), 4)
            pe.wait_ge(sem("bias_out"), 16)
            pe.wait_ge(acc_free, first_acc["zg"])
            scores2(0)
            scores2(1)
            for v in range(len(UNITS2)):
                if v + 2 < len(UNITS2):
                    scores2(v + 2)
                turn(64 + v, NT, 1)
                if v:
                    values2(v - 1)
            values2(len(UNITS2) - 1)
            pe.wait_ge(sem("pt_evac"), 96)
            for s in range(4):
                wh, wl = use_slab()
                for j in range(2):
                    feature_tile(wh, wl, 0, KD, slice(j * P, (j + 1) * P), (h_hi, h_lo))
                    if s < 2:
                        small_norm(18 + 2 * s + j)
            pe.wait_ge(sem("z_ready"), 8)
            for s in range(4):
                wh, wl = use_slab()
                for j in range(2):
                    feature_tile(wh, wl, 0, KD, slice(j * P, (j + 1) * P), (z_hi, z_lo))
            for t in range(NT):
                for half in range(2):
                    pe.wait_ge(acc_free, first_acc["wout2"] + 4 * half + 4)
                    o = open_acc()
                    for m in range(4):
                        ins = pe.transpose(o[:, m * P:(m + 1) * P], x[:, 4 * half + m, t * P:(t + 1) * P], ident)
                    close_acc(ins)

        @block.vector
        def _(dve):
            def done(ins, name="dve_seq"):
                dve.wait_ge(sem(name), tick(ins, name))

            acc_at = [0]

            def take():
                a = acc_at[0]
                acc_at[0] += 1
                dve.wait_ge(acc_full, a + 1)
                return bank[a % 4]

            def free(ins, n=1):
                ins.then_inc(acc_free, n)

            freed = lambda: dve.wait_ge(acc_free, acc_at[0])

            def copy_tile(dst, n=S):
                free(dve.tensor_copy(dst, take()[:, 0:n]))

            def add_square(n, k):
                dve.wait_ge(sem("nsq"), 8 * n + k + 1)
                dve.wait_ge(sem("dve_seq"), count.get("dve_seq", 0))
                if k > 1:
                    dve.wait_ge(sem("sq_added"), 7 * n + k - 1)
                ins = dve.tensor_add(sqsum[:, :], (sq[0] if k == 1 else sqsum)[:, :], sq[k % 2][:, :])
                done(ins, "sq_added")
                if n == 3:
                    dve.wait_ge(sem("nsqg"), k + 1)
                    done(dve.tensor_add(sqgsum[:, :], (sqg[0] if k == 1 else sqgsum)[:, :], sqg[k % 2][:, :]), "sqg_added")
                if k == KD - 1:
                    done(dve.memset(mstat[:, 0, 7:8], 0.0), "sq_sum")

            def squares_from(n, k):
                for i in range(k, KD):
                    add_square(n, i)

            def final_tile(k):
                done(dve.scalar_tensor_tensor(x[:, k, :], x[:, k, :], col[:, G_FIN + k:G_FIN + k + 1], rs[:, :], ALU.mult, ALU.mult))

            def big_norm(n, gains):
                dve.wait_ge(sem("nstd"), n + 1)
                done(dve.reciprocal(rs[:, :], std[:, :]), "rs_ready")
                if n == 3:
                    dve.wait_ge(sem("gmm"), 1)
                    done(dve.tensor_mul(tmp[:, :], bank[6][:, :], rs[:, :]))
                    done(dve.tensor_mul(tmp[:, :], tmp[:, :], rs[:, :]), "gsum_ready")
                    final_tile(0)
                    dve.wait_ge(sem("nstd"), 5)
                    done(dve.reciprocal(rs2[:, :], std[:, :]), "rs_ready")

            def make_h(n, gains, shift=None):
                def low(k):
                    dve.wait_ge(sem("h_hi_ready"), n * KD + k + 1)
                    tick(dve.tensor_sub(h_lo[:, k, :], (tmp, tmp2)[k % 2][:, :], h_hi[:, k, :]), "h_ready")
                for k in range(KD):
                    t = (tmp, tmp2)[k % 2][:, :]
                    if k >= 2:
                        dve.wait_ge(sem("h_ready"), n * KD + k - 1)
                    if n == 3 and k:
                        final_tile(k)
                    ins = dve.scalar_tensor_tensor(t, x[:, k, :], col[:, gains + k:gains + k + 1], (rs2 if n == 3 else rs)[:, :], ALU.mult, ALU.mult)
                    if shift is not None:
                        done(ins)
                        ins = dve.tensor_scalar(t, t, col[:, shift + k:shift + k + 1], None, ALU.add)
                    tick(ins, "hn_ready")
                    if k:
                        low(k - 1)
                low(KD - 1)
                dve.wait_ge(sem("h_ready"), (n + 1) * KD)

            def rope(src, cos, sin, dsts, n=None):
                j = count.get("rope_done", 0)
                w = tmp[:, :] if n is None else tmp[:, 0:n]
                w2_ = tmp2[:, :] if n is None else tmp2[:, 0:n]
                b = rope_bank(j)[:, :] if n is None else rope_bank(j)[:, 0:n]
                if n is not None:
                    w, w2_, b = (z.rearrange("p (g n) -> p g n", g=GROUPS)[:, :, 0:NCMP] for z in (w, w2_, b))
                done(dve.tensor_mul(w, src, cos))
                dve.wait_ge(sem("rope_mm"), j + 1)
                done(dve.tensor_mul(w2_, b, sin))
                for i, (dst, r) in enumerate(dsts):
                    ins = dve.tensor_add(dst, w[r[0]:r[1]], w2_[r[0]:r[1]])
                    done(ins, "rope_done" if i == len(dsts) - 1 else "dve_seq")

            def small_norm(j):
                dve.wait_ge(sem("sstd"), j + 1)
                done(dve.reciprocal(rs[:, :], std[:, :]), "rs_ready")

                def scaled(dst, src, g, r=(0, P), name="dve_seq"):
                    done(dve.scalar_tensor_tensor(dst, src, col[r[0]:r[1], g:g + 1], rs[r[0]:r[1], :], ALU.mult, ALU.mult), name)

                if j < 2:
                    for k in (range(2) if j == 0 else (2,)):
                        src = cqt[:, k, :] if j == 0 else ckr[:, 0, :]
                        scaled(tmp[:, :], src, G_QA + k)
                        done(dve.tensor_copy(c_hi[:, k, :], tmp[:, :]))
                        done(dve.tensor_sub(c_lo[:, k, :], tmp[:, :], c_hi[:, k, :]), "c_split")
                elif j < 6:
                    scaled(dq[:, j - 2, :], dq[:, j - 2, :], G_DQ)
                elif j < 10:
                    for e in range(2):
                        q = slice(64 * e, 64 * e + 64)
                        scaled(dkz[q, 2 * (j - 6) + e, :], dk[q, j - 6, :], G_DK, (64 * e, 64 * e + 64))
                elif j < 14:
                    h = j - 10
                    e = 64 * (h % 2)
                    scaled(qm[:, h, :], qm[:, h, :], G_QN)
                    scaled(qm[e:e + 64, 4 + h // 2, :], qm[e:e + 64, 4 + h // 2, :], G_QP, (e, e + 64), "qpe_ready")
                elif j < 18:
                    h = j - 14
                    e = 64 * (h % 2)
                    scaled(kn[:, h, :], kn[:, h, :], G_KN)
                    scaled(kpz[e:e + 64, h, :], ckr[e:e + 64, 1, :], G_KP, (e, e + 64), "kpe_ready")
                else:
                    scaled(diff_out[j - 18], diff_out[j - 18], G_SUB)

            done(dve.memset(col[:, G_EPS:G_EPS + 1], EPS), "eps_set")
            done(dve.memset(col[:, G_GNEPS:G_GNEPS + 1], GN_EPS), "eps_set")
            for k in range(KD):
                copy_tile(x[:, k, :])
                if k >= 2:
                    add_square(0, k - 1)
            squares_from(0, KD - 1)
            dve.wait_ge(sem("col_landed"), 16 * N_COL_DMAS)
            freed()
            big_norm(0, G_F1)
            make_h(0, G_F1)

            def modulate(i):
                half = ada_sum[:, 1536 * (i % 2):1536 * (i % 2) + 1536]
                if i == 0:
                    dve.wait_ge(sem("c_silu"), 1)
                dve.wait_ge(sem(f"ada_landed{i % 3}"), 16 * (i // 3 + 1))
                if i >= 2:
                    dve.wait_ge(sem("ada_used"), i - 1)
                    tick(dve.scalar_tensor_tensor(half, ada_w[i % 3][:, :], sc_f[:, i // 2:i // 2 + 1], half, ALU.mult, ALU.add), "ada_used")
                else:
                    tick(dve.tensor_scalar(half, ada_w[i % 3][:, :], sc_f[:, 0:1], None, ALU.mult), "ada_used")

            def prepare(m):
                if m == 0:
                    done(dve.memset(lamt[:, :], 0.0))
                    for i in range(2):
                        done(dve.tensor_mul(lamt[0:64, i:i + 1], col[0:64, G_LAM + 2 * i:G_LAM + 2 * i + 1], col[0:64, G_LAM + 2 * i + 1:G_LAM + 2 * i + 2]),
                             "lam_prod" if i else "dve_seq")
                if m == 1:
                    dve.wait_ge(sem("pos_landed"), 48)
                    done(dve.tensor_copy(posb, posi[:, :]))
                    done(dve.tensor_single_scalar(poci[:, :], poci[:, :], -64, ALU.bitwise_and))
                    done(dve.tensor_copy(lim, poci[:, :]))
                    done(dve.tensor_scalar(lim, lim, 64.0, None, ALU.add))
                if m == 2:
                    a0, a1, a2, a3 = (z[:, :] for z in ang)
                    done(dve.tensor_scalar(a0, posb, cst[:, C_MISC + 1:C_MISC + 2], None, ALU.mult))
                    done(dve.tensor_scalar(a1, a0, 1.0 / (2 * math.pi), None, ALU.mult))
                    done(dve.tensor_scalar(a1, a1, 12582912.0, None, ALU.add))
                    done(dve.tensor_scalar(a1, a1, 12582912.0, None, ALU.subtract))
                    for part in TURN:
                        done(dve.scalar_tensor_tensor(a0, a1, -part, a0, ALU.mult, ALU.add))
                    done(dve.tensor_scalar(a1, a0, math.pi / 2, None, ALU.add))
                    done(dve.tensor_scalar(a2, a1, math.pi, -2 * math.pi, ALU.is_gt, ALU.mult))
                    done(dve.tensor_add(a1, a1, a2))
                    for z in (a0, a1):
                        ins = dve.tensor_scalar(z, z, PI32, -PI32, ALU.min, ALU.max)
                        done(ins, "ang_ready" if z is a1 else "dve_seq")
                if m == 3:
                    for q in range(4):
                        r = slice(32 * q, 32 * q + 32)
                        done(dve.tensor_scalar(thr[r, :], posb[r, q:S:4], cst[r, C_MISC:C_MISC + 1], None, ALU.add))
                if m == 4:
                    dve.wait_ge(sem("dcol_full"), 1)
                    done(dve.tensor_copy(dcol[:, :], bank[4][:, 0:4]))
                    done(dve.memset(wf[:, :], 0.0))
                    for q in range(4):
                        done(dve.tensor_copy(wf[32 * q:32 * q + 32, 112 + 4 * q:116 + 4 * q], dcol[32 * q:32 * q + 32, :]))
                    done(dve.tensor_copy(win_hi[:, :], wf[:, :]))
                    done(dve.tensor_sub(win_lo[:, :], wf[:, :], win_hi[:, :]), "win_ready")
                if m == 5:
                    dve.wait_ge(sem("lam_exp"), 1)
                    done(dve.tensor_sub(lamt[:, 4:5], lamt[:, 3:4], lamt[:, 2:3]))
                    done(dve.tensor_scalar(neglam, lamt[:, 4:5], LAM_INIT, None, ALU.subtract))
                    done(dve.tensor_scalar(col[:, G_SUB:G_SUB + 1], col[:, G_SUB:G_SUB + 1], 1.0 - LAM_INIT, None, ALU.mult))

            def ffn(f, n):
                for half in range(2):
                    for m in range(HALF_F):
                        i = count.get("hid_ready", 0)
                        take()
                        up = take()
                        dve.wait_ge(sem("act_gate"), i + 1)
                        free(dve.tensor_mul(act_f[:, :], silu[i % 2][:, :], up[:, :]), 2)
                        freed()
                        done(dve.tensor_copy(u_hi[:, m, :], act_f[:, :]))
                        done(dve.tensor_sub(u_lo[:, m, :], act_f[:, :], u_hi[:, m, :]), "hid_ready")
                        if f == "ffn2" and half == 0:
                            prepare(m)
                        if f == "ffn1" and half == 0:
                            modulate(m)
                    if f == "ffn1" and half:
                        dve.wait_ge(sem("ada_full"), 1)
                        done(dve.tensor_add(col[:, G_MOD:G_MOD + 24], bank[7][:, 0:24], col[:, G_ADAB:G_ADAB + 24]))
                        done(dve.scalar_tensor_tensor(col[:, G_MOD + 8:G_MOD + 16], col[:, G_MOD + 8:G_MOD + 16], 1.0, col[:, G_N2:G_N2 + 8], ALU.add, ALU.mult), "mod_ready")
                    for m in range(KD):
                        free(dve.scalar_tensor_tensor(x[:, m, :], take()[:, :], 0.5, x[:, m, :], ALU.mult, ALU.add))
                        if half and m >= 2:
                            add_square(n, m - 1)
                        if f == "ffn1" and half == 0 and HALF_F + m < 16:
                            modulate(HALF_F + m)
                    freed()
                squares_from(n, KD - 1)

            ffn("ffn1", 1)
            dve.wait_ge(sem("const_landed"), 16)
            big_norm(1, G_MIX)
            make_h(1, G_MIX)
            cosN, sinN = cst[:, C_COSN:C_COSN + S], cst[:, C_SINN:C_SINN + S]
            done(dve.memset(kz[:, :, :, :, :].rearrange("p i g e s -> p (i g e s)"), 0.0))
            done(dve.memset(kcz[:, :, :, :].rearrange("p e g n -> p (e g n)"), 0.0))

            def rope_key(i):
                rope(kv_s[:, i, :], cosN, sinN,
                     [(kz[64 * e:64 * e + 64, i, g, e, :], (64 * g, 64 * g + 64)) for g in range(GROUPS) for e in range(2)])

            for j in range(12):
                copy_tile((qT[:, j, :] if j < 8 else (kv_c, kv_s)[(j - 8) // 2][:, j % 2, :]))
                freed()
                if 1 <= j <= 8:
                    rope(qT[:, j - 1, :], cosN, sinN, [(qT[:, j - 1, :], (0, P))])
                if j == 9:
                    for i in range(2):
                        for g in range(GROUPS):
                            q = 64 * g
                            tick(dve.tensor_copy(T2[0:64, i, g, :], kv_c[q:q + 64, i, :]), "T2_ready")
                            tick(dve.tensor_copy(T2[64:128, i, g, 0:S - 1], kv_c[q:q + 64, i, 1:S]), "T2_ready")
                if j == 11:
                    rope_key(0)
            for t in range(NT):
                copy_tile(vtok[:, t, :], 256)
                if t == 0:
                    rope_key(1)
            for t in range(NT):
                take()
                dve.wait_ge(sem("gates_ready"), t + 1)
                free(dve.memset(mstat[:, 0, 0:1], 0.0))
                freed()
            done(dve.memset(hidT[:, :, :, :, :], 0.0))
            dve.wait_ge(sem("posT_full"), 1)
            done(dve.tensor_copy(posT[:, :], bank[4][:, 0:16]), "posT_ready")
            for i in range(2):
                dve.wait_ge(sem("cmp_hid"), i + 1)
                hx = hid[:, i, :]
                done(dve.tensor_copy(hx, bank[6 + i][0:NROW, 0:256]))
                done(dve.tensor_mul(gl[0][:, :], hx, hx))
                done(dve.tensor_scalar(gl[0][:, :], gl[0][:, :], 0.044715, 1.0, ALU.mult, ALU.add))
                done(dve.tensor_mul(gl[0][:, :], gl[0][:, :], hx), "gelu_in")
                dve.wait_ge(sem("gelu_tanh"), i + 1)
                done(dve.scalar_tensor_tensor(hx, gl[1][:, :], 1.0, hx, ALU.add, ALU.mult), "hid_cmp_ready")
            dve.wait_ge(sem("hidT_full"), 1)
            done(dve.tensor_scalar(hidT[:, :, :, :, 0:NCMP].rearrange("p i c g n -> p (i c) g n"),
                                   bank[4][:, 0:256].rearrange("p (a g n) -> p a g n", g=2, n=NCP)[:, :, :, 0:NCMP],
                                   0.5, None, ALU.mult))
            for j in range(4):
                done(dve.tensor_copy(hrep[:, :, :, j, :], hidT[:, 1, :, :, :]), "hidT_ready")
            dve.wait_ge(sem("cmp_kv"), 1)
            done(dve.memset(vcz[:, :, :, :], 0.0))
            for j in range(4):
                q = slice(32 * j, 32 * j + 32)
                done(dve.tensor_copy(vcz[q, j, :, :], bank[5][q, 128:256].rearrange("p (g d) -> p g d", g=2)))
            done(dve.tensor_copy(kcr[:, :, :], bank[5][:, 0:64].rearrange("p (g n) -> p g n", g=2)), "kcr_ready")
            ends = [cst[:, c + 31:c + S:16].unsqueeze(1).to_broadcast([P, GROUPS, NCMP]) for c in (C_COSN, C_SINN)]
            rope(kcr[:, :, 0:NCMP], ends[0], ends[1], [(kcz[64 * e:64 * e + 64, e, :, 0:NCMP], (64 * e, 64 * e + 64)) for e in range(2)], 64)
            dve.wait_ge(sem("gates_ready"), 4)
            for t in range(NT):
                wide = lambda ap: ap.unsqueeze(2).to_broadcast([P, HEADS, NCP])
                seen = cst[:, C_CM01 + t * NCP:C_CM01 + (t + 1) * NCP].unsqueeze(1).to_broadcast([P, HEADS, NCP])
                add = cst[:, C_CADD + t * NCP:C_CADD + (t + 1) * NCP].unsqueeze(1).to_broadcast([P, HEADS, NCP])
                dve.wait_ge(sem("cmp_s"), t + 1)
                if t:
                    dve.wait_ge(sem("cmp_t"), t)
                done(dve.tensor_add(sc[:, :, :], bank[6 + t % 2][:, :].rearrange("p (h n) -> p h n", h=HEADS), add))
                done(dve.reduce_max(sstat[:, 0, :], sc[:, :, :], AX))
                done(dve.tensor_sub(sc[:, :, :], sc[:, :, :], wide(sstat[:, 0, :])), "cmp_in")
                dve.wait_ge(sem("cmp_exp"), t + 1)
                done(dve.tensor_mul(sc[:, :, :], sc[:, :, :], seen))
                done(dve.reduce_sum(sstat[:, 1, :], sc[:, :, :], AX))
                done(dve.tensor_scalar(sstat[:, 1, :], sstat[:, 1, :], 1e-20, None, ALU.max))
                done(dve.reciprocal(sstat[:, 2, :], sstat[:, 1, :]))
                done(dve.tensor_mul(sstat[:, 2, :], sstat[:, 2, :], gates[:, t, 0:48:3]))
                done(dve.tensor_mul(sc[:, :, :], sc[:, :, :], wide(sstat[:, 2, :])), "cmp_p")
                dve.wait_ge(sem("cmp_t"), t + 1)
                done(dve.tensor_copy(pTc[:, t, :, :], bank[4 + t % 2][:, :].rearrange("p (j q) -> p j q", j=4)), "cmp_pT")

            caus = cst[:, C_CAUS:C_CAUS + P]

            def peaks(u):
                t = UNITS[u][1]
                dve.wait_ge(sem("s_full"), u + 1)
                for i in range(2):
                    d = bank[2 * (u % 2) + i][:, t * P:(t + 1) * P]
                    ins = dve.tensor_add(d, d, caus)
                    tick(ins, "dve_seq")
                dve.wait_ge(sem("dve_seq"), count["dve_seq"])
                for i in range(2):
                    tick(dve.reduce_max(mstat[:, u % 2, i:i + 1], bank[2 * (u % 2) + i][:, 0:(t + 1) * P], AX), "dve_seq")
                dve.wait_ge(sem("dve_seq"), count["dve_seq"])
                tick(dve.tensor_scalar(mstat[:, u % 2, 2:4], mstat[:, u % 2, 0:2], -SCALE, None, ALU.mult), "nm_ready")

            def weigh(u):
                hp, t, e = UNITS[u]
                h, n = 2 * hp + e, (t + 1) * P
                dve.wait_ge(sem("p_exp"), u + 1)
                done(dve.reciprocal(mstat[:, u % 2, 6:8], mstat[:, u % 2, 4:6]))
                done(dve.tensor_mul(mstat[:, u % 2, 6:8], mstat[:, u % 2, 6:8], gates[:, t, 3 * h + 1:3 * h + 3]))
                for i in range(2):
                    p_ = Pm[u % 2][:, i, 0:n]
                    ins = dve.tensor_scalar(p_, p_, mstat[:, u % 2, 6 + i:7 + i], None, ALU.mult)
                tick(ins, "p_ready")

            def pair_out(hp):
                dve.wait_ge(sem("pv_done"), 8 * hp + 8)
                done(dve.tensor_copy(a_hi[:, hp, :], bank[6 + hp % 2][:, :]))
                done(dve.tensor_sub(a_lo[:, hp, :], bank[6 + hp % 2][:, :], a_hi[:, hp, :]), "o_free")

            peaks(0)
            peaks(1)
            for u in range(len(UNITS)):
                weigh(u)
                if u + 2 < len(UNITS):
                    peaks(u + 2)
                if u >= 9 and u % 8 == 1:
                    pair_out(u // 8 - 1)
            pair_out(7)
            cosR, sinR = cst[:, C_COSR:C_COSR + S], cst[:, C_SINR:C_SINR + S]
            done(dve.memset(rkz[:, :, :].rearrange("p h s -> p (h s)"), 0.0))

            def rope_r(j):
                if j < 4:
                    rope(rq[:, j, :], cosR, sinR, [(rq[:, j, :], (0, P))])
                else:
                    rope(rk[:, j - 4, :], cosR, sinR,
                         [(rkz[64 * e:64 * e + 64, 2 * (j - 4) + e, :], (64 * e, 64 * e + 64)) for e in range(2)])

            for j in range(8):
                copy_tile((rq, rk)[j // 4][:, j % 4, :])
                freed()
                if j:
                    rope_r(j - 1)
            for s in range(4):
                for t in range(NT):
                    copy_tile(rv[:, t, s * 256:(s + 1) * 256], 256)
                    if (s, t) == (0, 0):
                        rope_r(7)
            freed()
            for i in range(4 * RH):
                h, kb = i // 4, i % 4
                n = S - kb * P
                dve.wait_ge(sem("r_s"), i + 1)
                if kb == 0:
                    dve.wait_ge(sem(f"dec_landed{h % 2}"), 16 * (h // 2 + 1))
                if i >= 2:
                    dve.wait_ge(sem("r_pv"), i - 1)
                tick(dve.tensor_mul(rS[kb % 2][:, 0:n], bank[kb][:, 0:n], dec[h % 2][:, 0:n]), "r_m")
                if kb == 0 and h >= 1:
                    dve.wait_ge(sem("r_pv"), 4 * h)
                    tick(dve.tensor_copy(ro[:, h - 1, :], bank[6 + (h - 1) % 2][:, :]), "r_o")
            dve.wait_ge(sem("r_pv"), 4 * RH)
            done(dve.tensor_copy(ro[:, RH - 1, :], bank[6 + (RH - 1) % 2][:, :]), "r_o")
            for h in range(RH + 1):
                if h < RH:
                    dve.wait_ge(sem("ln1"), h + 1)
                    done(dve.scalar_tensor_tensor(ro[:, h, :], bank[4][:, :], -1.0 / P, ro[:, h, :], ALU.mult, ALU.add), "ln_c")
                if h:
                    m = h - 1
                    dve.wait_ge(sem("ln_t"), h)
                    done(dve.reciprocal(rout[:, :], rcen[:, :]), "ln_r")
                    done(dve.scalar_tensor_tensor(ro[:, m, :], ro[:, m, :], col[:, G_GN + m:G_GN + m + 1], rout[:, :], ALU.mult, ALU.mult))
                    take()
                    dve.wait_ge(sem("rg_ready"), h)
                    free(dve.tensor_mul(rout[:, :], ro[:, m, :], rsil[m % 2][:, :]))
                    freed()
                    done(dve.tensor_copy(r_hi[:, m, :], rout[:, :]))
                    done(dve.tensor_sub(r_lo[:, m, :], rout[:, :], r_hi[:, m, :]), "r_ready")
            for m in range(KD):
                take()
                b = take()
                dve.wait_ge(sem("sg_ready"), 2 * m + 1)
                free(dve.tensor_mul(mixed[:, m, :], sg[0][:, :], b[:, :]), 2)
                take()
                b = take()
                dve.wait_ge(sem("sg_ready"), 2 * m + 2)
                free(dve.tensor_mul(mt[:, :], sg[1][:, :], b[:, :]), 2)
                freed()
                done(dve.tensor_add(mixed[:, m, :], mixed[:, m, :], mt[:, :]))
            for m in range(KD):
                done(dve.tensor_copy(h_hi[:, m, :], mixed[:, m, :]))
                done(dve.tensor_sub(h_lo[:, m, :], mixed[:, m, :], h_hi[:, m, :]), "mh_ready")
            for m in range(KD):
                free(dve.tensor_add(x[:, m, :], take()[:, :], x[:, m, :]))
                if m >= 2:
                    add_square(2, m - 1)
            squares_from(2, KD - 1)
            freed()
            big_norm(2, G_F2)
            make_h(2, G_F2)
            ffn("ffn2", 3)
            big_norm(3, G_FIN)
            make_h(3, G_MOD + 8, G_MOD)

            def bias_steps(slot):
                for i in bias_groups(slot):
                    if i >= 4:
                        dve.wait_ge(sem("bmm"), i - 3)
                    tick(dve.tensor_scalar(step[i % 4][:, :], posb, thr[:, i:i + 1], None, ALU.is_ge), "step_ready")

            slot_at = [0]

            def beside():
                slot = slot_at[0]
                slot_at[0] += 1
                freed()
                if slot == 5:
                    rope(ckr[:, 1, :], cosM, sinM, [(ckr[:, 1, :], (0, P))])
                if slot in (19, 20):
                    rope(qm[:, slot - 15, :], cosM, sinM, [(qm[:, slot - 15, :], (0, P))])
                if slot == 26:
                    done(dve.memset(kpz[:, :, :].rearrange("p h s -> p (h s)"), 0.0))
                for j in NORM_SLOT.get(slot - 1, []):
                    small_norm(j)
                bias_steps(slot + 1)

            dve.wait_ge(sem("trig_ready"), 1)
            done(dve.memset(dkz[:, :, :].rearrange("p h s -> p (h s)"), 0.0))
            bias_steps(0)
            for j in range(2):
                copy_tile(cqt[:, j, :])
                beside()
            for j in range(2):
                copy_tile(ckr[:, j, :])
                beside()
            for j in range(8):
                copy_tile((dq, dk)[j // 4][:, j % 4, :])
                beside()
            dve.wait_ge(sem("bmm"), P)
            for i in range(2):
                dve.wait_ge(sem(f"bias_stored{i}"), 128)
            for j in range(6):
                copy_tile(qm[:, j, :])
                beside()
            for j in range(4):
                copy_tile(kn[:, j, :])
                beside()
            for t in range(NT):
                copy_tile(vm[:, t, :])
                beside()
            for s in range(2):
                for t in range(NT):
                    copy_tile(dv[:, t, s * 256:(s + 1) * 256], 256)
                    beside()

            def peaks2(v):
                kind, h, t = UNITS2[v]
                u = 64 + v
                maps = 2 - kind
                if kind == 0:
                    dve.wait_ge(sem("bias_ready"), v - 15)
                add = hidden[t] if kind else bias[:, t, :]
                dve.wait_ge(sem("s_full"), u + 1)
                for i in range(maps):
                    d = bank[2 * (u % 2) + i][:, :]
                    tick(dve.scalar_tensor_tensor(d, d, (SCALE, MLA_SCALE)[kind], add, ALU.mult, ALU.add), "dve_seq")
                dve.wait_ge(sem("dve_seq"), count["dve_seq"])
                for i in range(maps):
                    tick(dve.reduce_max(mstat[:, u % 2, i:i + 1], bank[2 * (u % 2) + i][:, :], AX), "dve_seq")
                dve.wait_ge(sem("dve_seq"), count["dve_seq"])
                tick(dve.tensor_scalar(mstat[:, u % 2, 2:2 + maps], mstat[:, u % 2, 0:maps], -1.0, None, ALU.mult), "nm_ready")

            def weigh2(v):
                kind = UNITS2[v][0]
                u, maps = 64 + v, 2 - UNITS2[v][0]
                st = mstat[:, u % 2, :]
                dve.wait_ge(sem("p_exp"), u + 1)
                done(dve.reciprocal(st[:, 6:6 + maps], st[:, 4:4 + maps]))
                p0 = Pm[u % 2][:, 0, :]
                if kind == 0:
                    p1 = Pm[u % 2][:, 1, :]
                    done(dve.tensor_scalar(p1, p1, st[:, 7:8], neglam, ALU.mult, ALU.mult))
                    tick(dve.scalar_tensor_tensor(p0, p0, st[:, 6:7], p1, ALU.mult, ALU.add), "p_ready")
                else:
                    tick(dve.tensor_scalar(p0, p0, st[:, 6:7], None, ALU.mult), "p_ready")

            def head_out(i):
                dve.wait_ge(sem("pv_done"), 64 + 4 * i + 4)
                done(dve.tensor_copy((latent_out + diff_out)[i], bank[6 + i % 2][:, :]), "o_free")

            for t in range(NT):
                done(dve.tensor_scalar(hidden[t], posb, lim[:, t:t + 1], NEG, ALU.is_ge, ALU.mult), "hidden_ready" if t == 3 else "dve_seq")
            peaks2(0)
            peaks2(1)
            for v in range(len(UNITS2)):
                weigh2(v)
                if v + 2 < len(UNITS2):
                    peaks2(v + 2)
                if v >= 5 and v % 4 == 1:
                    head_out(v // 4 - 1)
            head_out(7)
            for m in range(KD):
                if m < 4:
                    small_norm(18 + m)
                take()
                dve.wait_ge(sem("zg_ready"), m + 1)
                free(dve.tensor_mul(tmp[:, :], (diff_out + latent_out)[m], gate_out[m % 2][:, :]))
                freed()
                done(dve.tensor_copy(z_hi[:, m, :], tmp[:, :]))
                done(dve.tensor_sub(z_lo[:, m, :], tmp[:, :], z_hi[:, m, :]), "z_ready")
            for m in range(KD):
                free(dve.scalar_tensor_tensor(x[:, m, :], take()[:, :], col[:, G_MOD + 16 + m:G_MOD + 17 + m], x[:, m, :], ALU.mult, ALU.add))
            freed()
            for t in range(NT):
                for half in range(2):
                    copy_tile(osb[:, t, half * 512:(half + 1) * 512])


PI32 = 3.1415925
TURN = [6.28125, 0.0019340515136718750, 2 * math.pi - 6.28125 - 0.0019340515136718750]

IN_NAMES = ["x", "ffn1_norm", "ffn1_w_gate", "ffn1_w_up", "ffn1_w_down", "mix_norm", "w_in", "cmp_pos_emb",
            "cmp_k_w1", "cmp_k_w2", "cmp_v_w1", "cmp_v_w2", "ret_gn_gain", "w_branch_nsa", "w_branch_ret", "w_out",
            "ffn2_norm", "ffn2_w_gate", "ffn2_w_up", "ffn2_w_down", "final_norm", "c_2", "positions_2", "rel_bias_2",
            "ada_w_2", "ada_b_2", "norm_g_2", "w_in_2", "diff_q_norm_2", "diff_k_norm_2", "diff_lambda_2",
            "diff_sub_norm_2", "mla_q_a_norm_2", "mla_kv_a_norm_2", "w_uq_2", "w_uk_2", "w_uv_2", "mla_q_norm_2",
            "mla_k_norm_2", "w_out_2"]


def kernel(**inputs):
    import concourse.bacc as bacc
    from concourse.bass_utils import run_bass_kernel_spmd

    nc = bacc.Bacc("TRN2", target_bir_lowering=False, num_devices=1)
    arrays = {n: np.ascontiguousarray(inputs[n]) for n in IN_NAMES}
    arrays["consts"], arrays["decay"] = constants()
    aps = {n: nc.dram_tensor(f"in_{n}", a.shape, mybir.dt.from_np(a.dtype), kind="ExternalInput").ap() for n, a in arrays.items()}
    out = nc.dram_tensor("out", [1, S, D], F32, kind="ExternalOutput").ap()
    build(nc, aps, out)
    r = run_bass_kernel_spmd(nc, [{f"in_{n}": a for n, a in arrays.items()}], core_ids=[0])
    return r.results[0]["out"]
```
